# Optimizing a Trainium2 kernel written in Bass

```python
import jax
import jax.numpy as jnp
from jax import lax
import numpy as np
import math
import jax, jax.numpy as jnp

D_MODEL = 1024
BATCH = 1
SEQ = 512
DEPTH = 4

N_MIXERS = 3
N_MLA_LAYERS = (DEPTH + 2) // 3
N_SWA_LAYERS = (DEPTH + 1) // 3
N_FOX_LAYERS = DEPTH // 3
BLOCK = 128
NEG_INF = -1e30
RMS_EPS = 1e-6
LN_EPS = 1e-5
DEEPNORM_ALPHA = (2 * DEPTH) ** 0.25
DEEPNORM_BETA = (8 * DEPTH) ** -0.25

MLA_HEADS = 16
MLA_NOPE_DIM = 64
MLA_ROPE_DIM = 32
MLA_V_DIM = 64
MLA_Q_RANK = 384
MLA_KV_RANK = 256
ROPE_THETA = 10000.0
MLA_WIDTH = MLA_HEADS * MLA_V_DIM
MLA_IN = MLA_Q_RANK + MLA_KV_RANK + MLA_ROPE_DIM + MLA_WIDTH

SWA_Q_HEADS = 16
SWA_KV_HEADS = 4
SWA_GROUP = SWA_Q_HEADS // SWA_KV_HEADS
SWA_HEAD_DIM = 64
WINDOW = 128
SWA_WIDTH = SWA_Q_HEADS * SWA_HEAD_DIM
SWA_KV_WIDTH = SWA_KV_HEADS * SWA_HEAD_DIM
SWA_IN = 2 * SWA_WIDTH + 2 * SWA_KV_WIDTH

FOX_HEADS = 16
FOX_HEAD_DIM = 64
FOX_WIDTH = FOX_HEADS * FOX_HEAD_DIM
FOX_IN = 4 * FOX_WIDTH + FOX_HEADS


def _rmsnorm(x, g):
    xf = x.astype(jnp.float32)
    y = xf * lax.rsqrt(jnp.mean(xf * xf, axis=-1, keepdims=True) + RMS_EPS)
    return (y * g.astype(jnp.float32)).astype(x.dtype)

def _layernorm(x, g, b):
    xf = x.astype(jnp.float32)
    mu = jnp.mean(xf, axis=-1, keepdims=True)
    var = jnp.mean(jnp.square(xf - mu), axis=-1, keepdims=True)
    y = (xf - mu) * lax.rsqrt(var + LN_EPS) * g.astype(jnp.float32) + b.astype(jnp.float32)
    return y.astype(x.dtype)

def _rope_tables(seq, dim):
    inv = ROPE_THETA ** (-jnp.arange(0, dim, 2, dtype=jnp.float32) / dim)
    ang = jnp.arange(seq, dtype=jnp.float32)[:, None] * inv[None, :]
    return jnp.cos(ang), jnp.sin(ang)

def _apply_rope(x, cos, sin):
    x1, x2 = jnp.split(x.astype(jnp.float32), 2, axis=-1)
    return jnp.concatenate([x1 * cos - x2 * sin, x2 * cos + x1 * sin], axis=-1).astype(x.dtype)

def _alibi_slopes(n_heads):
    return 2.0 ** (-8.0 * jnp.arange(1, n_heads + 1, dtype=jnp.float32) / n_heads)

def _dense_causal(q, k, v, scale, cum=None):
    B, S, H, _ = q.shape
    dv = v.shape[-1]
    nb = S // BLOCK
    k_pos = jnp.arange(S)
    cum_t = None if cum is None else jnp.transpose(cum, (0, 2, 1))

    def one_block(n):
        start = n * BLOCK
        q_blk = lax.dynamic_slice_in_dim(q, start, BLOCK, axis=1)
        q_pos = start + jnp.arange(BLOCK)
        s = jnp.einsum('bqhd,bkhd->bhqk', q_blk, k, preferred_element_type=jnp.float32) * scale
        if cum_t is not None:
            c_q = lax.dynamic_slice_in_dim(cum_t, start, BLOCK, axis=2)
            s = s + c_q[..., :, None] - cum_t[:, :, None, :]
        s = jnp.where(k_pos[None, :] <= q_pos[:, None], s, NEG_INF)
        p = jax.nn.softmax(s, axis=-1).astype(v.dtype)
        return jnp.einsum('bhqk,bkhd->bqhd', p, v)

    out = lax.map(one_block, jnp.arange(nb))
    return jnp.transpose(out, (1, 0, 2, 3, 4)).reshape(B, S, H, dv)

def _mla_branch(x, w_in, q_norm, w_q_up, kv_norm, w_kv_up, w_out):
    B, S, _ = x.shape
    h = x @ w_in
    c1 = MLA_Q_RANK
    c2 = c1 + MLA_KV_RANK
    c3 = c2 + MLA_ROPE_DIM
    cq, ckv, k_rope, gate = h[..., :c1], h[..., c1:c2], h[..., c2:c3], h[..., c3:]
    q = (_rmsnorm(cq, q_norm) @ w_q_up).reshape(B, S, MLA_HEADS, MLA_NOPE_DIM + MLA_ROPE_DIM)
    kv = (_rmsnorm(ckv, kv_norm) @ w_kv_up).reshape(B, S, MLA_HEADS, MLA_NOPE_DIM + MLA_V_DIM)
    cos, sin = _rope_tables(S, MLA_ROPE_DIM)
    q_rope = _apply_rope(q[..., MLA_NOPE_DIM:], cos[:, None, :], sin[:, None, :])
    k_rope = _apply_rope(k_rope, cos, sin)
    q_full = jnp.concatenate([q[..., :MLA_NOPE_DIM], q_rope], axis=-1)
    k_full = jnp.concatenate(
        [kv[..., :MLA_NOPE_DIM],
         jnp.broadcast_to(k_rope[:, :, None, :], (B, S, MLA_HEADS, MLA_ROPE_DIM))], axis=-1)
    v = kv[..., MLA_NOPE_DIM:]
    scale = (MLA_NOPE_DIM + MLA_ROPE_DIM) ** -0.5
    o = _dense_causal(q_full, k_full, v, scale).reshape(B, S, MLA_WIDTH)
    return (o * jax.nn.silu(gate)) @ w_out

def _swa_branch(x, w_in, sinks, w_out):
    B, S, _ = x.shape
    nb = S // BLOCK
    h = x @ w_in
    c1 = SWA_WIDTH
    c2 = c1 + SWA_KV_WIDTH
    c3 = c2 + SWA_KV_WIDTH
    q = h[..., :c1].reshape(B, nb, BLOCK, SWA_KV_HEADS, SWA_GROUP, SWA_HEAD_DIM)
    k = h[..., c1:c2].reshape(B, nb, BLOCK, SWA_KV_HEADS, SWA_HEAD_DIM)
    v = h[..., c2:c3].reshape(B, nb, BLOCK, SWA_KV_HEADS, SWA_HEAD_DIM)
    gate = h[..., c3:]

    def band(t):
        prev = jnp.concatenate([jnp.zeros_like(t[:, :1]), t[:, :-1]], axis=1)
        return jnp.concatenate([prev, t], axis=2)

    kb, vb = band(k), band(v)
    scale = SWA_HEAD_DIM ** -0.5
    s = jnp.einsum('bnqkgd,bnskd->bnkgqs', q, kb, preferred_element_type=jnp.float32) * scale
    qi = jnp.arange(BLOCK)[:, None]
    kj = jnp.arange(2 * BLOCK)[None, :]
    dist = qi + BLOCK - kj
    key_pos = jnp.arange(nb)[:, None, None] * BLOCK - BLOCK + kj[None]
    valid = (dist >= 0) & (dist < WINDOW) & (key_pos >= 0)
    slopes = _alibi_slopes(SWA_Q_HEADS).reshape(SWA_KV_HEADS, SWA_GROUP)
    s = s - slopes[:, :, None, None] * dist.astype(jnp.float32)
    s = jnp.where(valid[None, :, None, None], s, NEG_INF)
    sink = sinks.astype(jnp.float32).reshape(SWA_KV_HEADS, SWA_GROUP)[:, :, None, None]
    m = jnp.maximum(jnp.max(s, axis=-1, keepdims=True), sink)
    p = jnp.exp(s - m)
    p = (p / (jnp.sum(p, axis=-1, keepdims=True) + jnp.exp(sink - m))).astype(vb.dtype)
    o = jnp.einsum('bnkgqs,bnskd->bnqkgd', p, vb).reshape(B, S, SWA_WIDTH)
    return (o * jax.nn.silu(gate)) @ w_out

def _fox_branch(x, w_in, b_f, w_out):
    B, S, _ = x.shape
    h = x @ w_in
    W = FOX_WIDTH
    q = h[..., :W].reshape(B, S, FOX_HEADS, FOX_HEAD_DIM)
    k = h[..., W:2 * W].reshape(B, S, FOX_HEADS, FOX_HEAD_DIM)
    v = h[..., 2 * W:3 * W].reshape(B, S, FOX_HEADS, FOX_HEAD_DIM)
    f_logit = h[..., 3 * W:3 * W + FOX_HEADS]
    gate = h[..., 3 * W + FOX_HEADS:]
    log_f = jax.nn.log_sigmoid(f_logit.astype(jnp.float32) + b_f.astype(jnp.float32))
    cum = jnp.cumsum(log_f, axis=1)
    o = _dense_causal(q, k, v, FOX_HEAD_DIM ** -0.5, cum).reshape(B, S, W)
    return (o * jax.nn.silu(gate)) @ w_out

def first_inputs(seed: int = 0) -> dict:
    key = jax.random.key(seed)
    ks = jax.random.split(key, 16)

    def nrm(k, shape, scale):
        return jax.random.normal(k, shape, jnp.float32) * scale

    return {
        "x": nrm(ks[0], (BATCH, SEQ, D_MODEL), 1.0),
        "ln_g": 1.0 + nrm(ks[1], (DEPTH, D_MODEL), 0.02),
        "ln_b": nrm(ks[2], (DEPTH, D_MODEL), 0.02),
        "mla_w_in": nrm(ks[3], (N_MLA_LAYERS, D_MODEL, MLA_IN), D_MODEL ** -0.5),
        "mla_q_norm": 1.0 + nrm(ks[4], (N_MLA_LAYERS, MLA_Q_RANK), 0.02),
        "mla_w_q_up": nrm(ks[5], (N_MLA_LAYERS, MLA_Q_RANK, MLA_HEADS * (MLA_NOPE_DIM + MLA_ROPE_DIM)), MLA_Q_RANK ** -0.5),
        "mla_kv_norm": 1.0 + nrm(ks[6], (N_MLA_LAYERS, MLA_KV_RANK), 0.02),
        "mla_w_kv_up": nrm(ks[7], (N_MLA_LAYERS, MLA_KV_RANK, MLA_HEADS * (MLA_NOPE_DIM + MLA_V_DIM)), MLA_KV_RANK ** -0.5),
        "mla_w_out": nrm(ks[8], (N_MLA_LAYERS, MLA_WIDTH, D_MODEL), DEEPNORM_BETA * MLA_WIDTH ** -0.5),
        "swa_w_in": nrm(ks[9], (N_SWA_LAYERS, D_MODEL, SWA_IN), D_MODEL ** -0.5),
        "swa_sinks": nrm(ks[10], (N_SWA_LAYERS, SWA_Q_HEADS), 0.5),
        "swa_w_out": nrm(ks[11], (N_SWA_LAYERS, SWA_WIDTH, D_MODEL), DEEPNORM_BETA * SWA_WIDTH ** -0.5),
        "fox_w_in": nrm(ks[12], (N_FOX_LAYERS, D_MODEL, FOX_IN), D_MODEL ** -0.5),
        "fox_b_f": jax.random.uniform(ks[13], (N_FOX_LAYERS, FOX_HEADS), jnp.float32, 1.0, 4.0),
        "fox_w_out": nrm(ks[14], (N_FOX_LAYERS, FOX_WIDTH, D_MODEL), DEEPNORM_BETA * FOX_WIDTH ** -0.5),
    }

def first_block(x, ln_g, ln_b, mla_w_in, mla_q_norm, mla_w_q_up, mla_kv_norm, mla_w_kv_up, mla_w_out,
              swa_w_in, swa_sinks, swa_w_out, fox_w_in, fox_b_f, fox_w_out):
    for i in range(DEPTH):
        j = i // N_MIXERS
        kind = i % N_MIXERS
        if kind == 0:
            y = _mla_branch(x, mla_w_in[j], mla_q_norm[j], mla_w_q_up[j], mla_kv_norm[j],
                            mla_w_kv_up[j], mla_w_out[j])
        elif kind == 1:
            y = _swa_branch(x, swa_w_in[j], swa_sinks[j], swa_w_out[j])
        else:
            y = _fox_branch(x, fox_w_in[j], fox_b_f[j], fox_w_out[j])
        x = _layernorm(DEEPNORM_ALPHA * x + y, ln_g[i], ln_b[i])
    return x


DEPTH_2 = 1

HEAD_DIM = 64
MIX_WIDTH = D_MODEL
GROUP_WIDTH = MIX_WIDTH // 4
CONV_WIDTH = 3
POOL_WINDOWS = (2, 4, 8, 16)
POOL_GROUP = GROUP_WIDTH // len(POOL_WINDOWS)
DSA_HEADS = GROUP_WIDTH // HEAD_DIM
IDX_HEADS = 8
IDX_DIM = 64
DSA_TOPK_MAX = 256
MOBA_HEADS = GROUP_WIDTH // HEAD_DIM
MOBA_BLOCK = 256
MOBA_TOPB_MAX = 3
REL_BUCKETS = 32
REL_MAX_DIST = 128
N_ATTN_HEADS = DSA_HEADS + MOBA_HEADS
D_FF = -(-8 * D_MODEL // (3 * 256)) * 256
PLE_DIM = 256
Q_BLOCK = 128
MOBA_Q_BLOCK = 64
SPLIT_SIZES = (GROUP_WIDTH, GROUP_WIDTH, GROUP_WIDTH,
               GROUP_WIDTH,
               GROUP_WIDTH, GROUP_WIDTH, GROUP_WIDTH, IDX_HEADS * IDX_DIM, IDX_DIM, IDX_HEADS,
               GROUP_WIDTH, GROUP_WIDTH, GROUP_WIDTH)
IN_COLS = sum(SPLIT_SIZES)


def rmsnorm(x, g):
    x32 = x.astype(jnp.float32)
    y = x32 * lax.rsqrt(jnp.mean(x32 * x32, axis=-1, keepdims=True) + RMS_EPS)
    return (y * g.astype(jnp.float32)).astype(x.dtype)

def rel_bucket(dist):
    n = jnp.maximum(dist, 0)
    max_exact = REL_BUCKETS // 2
    nf = jnp.maximum(n, 1).astype(jnp.float32)
    large = max_exact + (jnp.log(nf / max_exact) / math.log(REL_MAX_DIST / max_exact)
                         * (REL_BUCKETS - max_exact)).astype(jnp.int32)
    large = jnp.minimum(large, REL_BUCKETS - 1)
    return jnp.where(n < max_exact, n, large)

def short_conv_mixer(a_in, gate_c, gate_b, conv_w):
    h = gate_c * a_in
    y = lax.conv_general_dilated(h, conv_w[:, None, :].astype(h.dtype), window_strides=(1,),
                                 padding=[(CONV_WIDTH - 1, 0)],
                                 dimension_numbers=("NWC", "WIO", "NWC"),
                                 feature_group_count=h.shape[-1])
    return gate_b * y

def pool_mixer(v, pool_w, pool_scale):
    b, s, _ = v.shape
    v32 = v.astype(jnp.float32)
    cs = jnp.concatenate([jnp.zeros((b, 1, GROUP_WIDTH), jnp.float32), lax.cumsum(v32, axis=1)], axis=1)
    t = jnp.arange(s)
    outs = []
    for g, w in enumerate(POOL_WINDOWS):
        sl = slice(g * POOL_GROUP, (g + 1) * POOL_GROUP)
        c = cs[:, :, sl]
        upper = c[:, 1:]
        lower = jnp.concatenate([jnp.zeros((b, w - 1, POOL_GROUP), jnp.float32), c[:, :s + 1 - w]], axis=1)
        cnt = jnp.minimum(t + 1, w).astype(jnp.float32)[None, :, None]
        outs.append((upper - lower) / cnt - v32[:, :, sl])
    d = jnp.stack(outs, axis=2)
    y = jnp.einsum("bsgc,gcd->bsgd", d, pool_w.astype(jnp.float32)).reshape(b, s, GROUP_WIDTH)
    return (y * pool_scale.astype(jnp.float32)).astype(v.dtype)

def dsa_mixer(q, k, v, iq, ik, iw, bias_tab):
    b, s, nh, hd = q.shape
    topk = min(DSA_TOPK_MAX, s // 4)
    idx_scale = (IDX_HEADS ** -0.5) * (IDX_DIM ** -0.5)
    ik32 = ik.astype(jnp.float32)
    bidx = jnp.arange(b)[:, None, None]
    spos = jnp.arange(s)

    def chunk(c):
        t0 = c * Q_BLOCK
        tq = t0 + jnp.arange(Q_BLOCK)
        qc = lax.dynamic_slice_in_dim(q, t0, Q_BLOCK, axis=1).astype(jnp.float32)
        iqc = lax.dynamic_slice_in_dim(iq, t0, Q_BLOCK, axis=1).astype(jnp.float32)
        iwc = lax.dynamic_slice_in_dim(iw, t0, Q_BLOCK, axis=1).astype(jnp.float32)
        sc = jax.nn.relu(jnp.einsum("bqhd,bsd->bqhs", iqc, ik32))
        score = jnp.einsum("bqh,bqhs->bqs", iwc, sc) * idx_scale
        score = jnp.where(spos[None, None, :] <= tq[None, :, None], score, -jnp.inf)
        _, sel = lax.top_k(score, topk)
        valid = sel <= tq[None, :, None]
        kg = k[bidx, sel].astype(jnp.float32)
        vg = v[bidx, sel].astype(jnp.float32)
        logits = jnp.einsum("bqhd,bqkhd->bhqk", qc, kg) * (hd ** -0.5)
        bias = jnp.moveaxis(bias_tab.astype(jnp.float32)[:, rel_bucket(tq[None, :, None] - sel)], 0, 1)
        logits = jnp.where(valid[:, None], logits + bias, -jnp.inf)
        probs = jax.nn.softmax(logits, axis=-1)
        return jnp.einsum("bhqk,bqkhd->bqhd", probs, vg)

    out = lax.map(chunk, jnp.arange(s // Q_BLOCK))
    return out.transpose(1, 0, 2, 3, 4).reshape(b, s, nh * hd).astype(q.dtype)

def moba_mixer(q, k, v, bias_tab):
    b, s, nh, hd = q.shape
    nb = -(-s // MOBA_BLOCK)
    pad = nb * MOBA_BLOCK - s
    kp = jnp.pad(k, ((0, 0), (0, pad), (0, 0), (0, 0)))
    vp = jnp.pad(v, ((0, 0), (0, pad), (0, 0), (0, 0)))
    kblk = kp.reshape(b, nb, MOBA_BLOCK, nh, hd)
    kmean = jnp.mean(kblk.astype(jnp.float32), axis=2)
    kblk_t = kblk.transpose(0, 3, 1, 2, 4)
    vblk_t = vp.reshape(b, nb, MOBA_BLOCK, nh, hd).transpose(0, 3, 1, 2, 4)
    topb = min(MOBA_TOPB_MAX, nb - 1)
    scale = hd ** -0.5
    tab = bias_tab.astype(jnp.float32)
    bi = jnp.arange(b)[:, None, None, None]
    hi = jnp.arange(nh)[None, :, None, None]
    blk_off = jnp.arange(MOBA_BLOCK)

    def chunk(c):
        t0 = c * MOBA_Q_BLOCK
        tq = t0 + jnp.arange(MOBA_Q_BLOCK)
        ob = t0 // MOBA_BLOCK
        qc = lax.dynamic_slice_in_dim(q, t0, MOBA_Q_BLOCK, axis=1).astype(jnp.float32)
        ko = lax.dynamic_slice_in_dim(kp, ob * MOBA_BLOCK, MOBA_BLOCK, axis=1).astype(jnp.float32)
        vo = lax.dynamic_slice_in_dim(vp, ob * MOBA_BLOCK, MOBA_BLOCK, axis=1).astype(jnp.float32)
        spos_o = ob * MOBA_BLOCK + blk_off
        lo = jnp.einsum("bqhd,bshd->bhqs", qc, ko) * scale + tab[:, rel_bucket(tq[:, None] - spos_o[None, :])][None]
        lo = jnp.where((spos_o[None, :] <= tq[:, None])[None, None], lo, -jnp.inf)
        if topb == 0:
            po = jax.nn.softmax(lo, axis=-1)
            return jnp.einsum("bhqs,bshd->bqhd", po, vo)
        gate = jnp.einsum("bqhd,bnhd->bhqn", qc, kmean)
        gate = jnp.where(jnp.arange(nb)[None, None, None, :] < ob, gate, -jnp.inf)
        _, sel = lax.top_k(gate, topb)
        valid = sel < ob
        kg = kblk_t[bi, hi, sel].astype(jnp.float32)
        vg = vblk_t[bi, hi, sel].astype(jnp.float32)
        lp = jnp.einsum("bqhd,bhqnsd->bhqns", qc, kg) * scale
        spos_p = sel[..., None] * MOBA_BLOCK + blk_off
        lp = lp + tab[hi[..., None], rel_bucket(tq[None, None, :, None, None] - spos_p)]
        lp = jnp.where(valid[..., None], lp, -jnp.inf)
        npast = topb * MOBA_BLOCK
        logits = jnp.concatenate([lp.reshape(b, nh, MOBA_Q_BLOCK, npast), lo], axis=-1)
        probs = jax.nn.softmax(logits, axis=-1)
        pp = probs[..., :npast].reshape(b, nh, MOBA_Q_BLOCK, topb, MOBA_BLOCK)
        po = probs[..., npast:]
        return (jnp.einsum("bhqns,bhqnsd->bqhd", pp, vg) + jnp.einsum("bhqs,bshd->bqhd", po, vo))

    out = lax.map(chunk, jnp.arange(s // MOBA_Q_BLOCK))
    return out.transpose(1, 0, 2, 3, 4).reshape(b, s, nh * hd).astype(q.dtype)

def swiglu(h, w_gate_up, w_down):
    gu = h @ w_gate_up
    gate, up = jnp.split(gu, 2, axis=-1)
    return (jax.nn.silu(gate) * up) @ w_down

def second_inputs(seed: int = 0) -> dict:
    key = jax.random.key(seed)
    ks = jax.random.split(key, 20)
    f32 = jnp.float32

    def nrm(k, shape, scale):
        return jax.random.normal(k, shape, f32) * scale

    def gain(k, shape):
        return 1.0 + 0.05 * jax.random.normal(k, shape, f32)

    return {
        "x": nrm(ks[0], (BATCH, SEQ, D_MODEL), 1.0),
        "p": nrm(ks[1], (DEPTH_2, BATCH, SEQ, PLE_DIM), 1.0),
        "rel_bias": nrm(ks[2], (N_ATTN_HEADS, REL_BUCKETS), 0.5),
        "g_mix_pre": gain(ks[3], (DEPTH_2, D_MODEL)),
        "w_in": nrm(ks[4], (DEPTH_2, D_MODEL, IN_COLS), D_MODEL ** -0.5),
        "conv_w": nrm(ks[5], (DEPTH_2, CONV_WIDTH, GROUP_WIDTH), CONV_WIDTH ** -0.5),
        "pool_w": nrm(ks[6], (DEPTH_2, len(POOL_WINDOWS), POOL_GROUP, POOL_GROUP), POOL_GROUP ** -0.5),
        "pool_scale": gain(ks[7], (DEPTH_2, GROUP_WIDTH)),
        "w_out": nrm(ks[8], (DEPTH_2, MIX_WIDTH, D_MODEL), MIX_WIDTH ** -0.5),
        "g_mix_post": gain(ks[9], (DEPTH_2, D_MODEL)),
        "g_ffn_pre": gain(ks[10], (DEPTH_2, D_MODEL)),
        "w_gate_up": nrm(ks[11], (DEPTH_2, D_MODEL, 2 * D_FF), D_MODEL ** -0.5),
        "w_down": nrm(ks[12], (DEPTH_2, D_FF, D_MODEL), D_FF ** -0.5),
        "g_ffn_post": gain(ks[13], (DEPTH_2, D_MODEL)),
        "g_ple": gain(ks[14], (DEPTH_2, D_MODEL)),
        "w_ple_gate": nrm(ks[15], (DEPTH_2, D_MODEL, D_MODEL), D_MODEL ** -0.5),
        "w_ple_proj": nrm(ks[16], (DEPTH_2, PLE_DIM, D_MODEL), PLE_DIM ** -0.5),
    }

def second_block(x, p, rel_bias, g_mix_pre, w_in, conv_w, pool_w, pool_scale, w_out, g_mix_post,
              g_ffn_pre, w_gate_up, w_down, g_ffn_post, g_ple, w_ple_gate, w_ple_proj):
    b, s, _ = x.shape
    split_at = tuple(int(o) for o in np.cumsum(SPLIT_SIZES)[:-1])

    def heads(t):
        return t.reshape(b, s, -1, HEAD_DIM)

    for i in range(DEPTH_2):
        h = rmsnorm(x, g_mix_pre[i])
        z = h @ w_in[i]
        (a_in, a_c, a_b, pv, cq, ck, cv, iq, ik, iw, dq, dk, dv) = jnp.split(z, split_at, axis=-1)
        ya = short_conv_mixer(a_in, a_c, a_b, conv_w[i])
        yb = pool_mixer(pv, pool_w[i], pool_scale[i])
        yc = dsa_mixer(heads(cq), heads(ck), heads(cv), iq.reshape(b, s, IDX_HEADS, IDX_DIM), ik, iw,
                       rel_bias[:DSA_HEADS])
        yd = moba_mixer(heads(dq), heads(dk), heads(dv), rel_bias[DSA_HEADS:])
        mix = jnp.concatenate([ya, yb, yc, yd], axis=-1) @ w_out[i]
        x = x + rmsnorm(mix, g_mix_post[i])
        f = swiglu(rmsnorm(x, g_ffn_pre[i]), w_gate_up[i], w_down[i])
        x = x + rmsnorm(f, g_ffn_post[i])
        gate = jax.nn.sigmoid(rmsnorm(x, g_ple[i]) @ w_ple_gate[i])
        x = x + gate * (p[i] @ w_ple_proj[i])
    return x


def setup_inputs(seed=0):
    out = dict(first_inputs(seed))
    for name, value in second_inputs(seed + 1).items():
        if name != "x":
            out[name + "_2"] = value
    return out


def reference(
    x, ln_g, ln_b, mla_w_in, mla_q_norm, mla_w_q_up, mla_kv_norm, mla_w_kv_up, mla_w_out,
    swa_w_in, swa_sinks, swa_w_out, fox_w_in, fox_b_f, fox_w_out, p_2, rel_bias_2, g_mix_pre_2,
    w_in_2, conv_w_2, pool_w_2, pool_scale_2, w_out_2, g_mix_post_2, g_ffn_pre_2, w_gate_up_2,
    w_down_2, g_ffn_post_2, g_ple_2, w_ple_gate_2, w_ple_proj_2,
):
    x = first_block(
        x, ln_g, ln_b, mla_w_in, mla_q_norm, mla_w_q_up, mla_kv_norm, mla_w_kv_up, mla_w_out,
        swa_w_in, swa_sinks, swa_w_out, fox_w_in, fox_b_f, fox_w_out,
    )
    return second_block(
        x, p_2, rel_bias_2, g_mix_pre_2, w_in_2, conv_w_2, pool_w_2, pool_scale_2, w_out_2,
        g_mix_post_2, g_ffn_pre_2, w_gate_up_2, w_down_2, g_ffn_post_2, g_ple_2, w_ple_gate_2,
        w_ple_proj_2,
    )


_drawn_inputs = setup_inputs


def setup_inputs(seed=0):
    import zlib

    import numpy as np

    out = dict(_drawn_inputs(seed))
    spreads = {}
    factors = {'mla_q_norm': 8.0, 'mla_kv_norm': 8.0, 'swa_sinks': 7.72, 'g_ple_2': 23.548}
    for name, (base, spread) in spreads.items():
        noise = np.random.default_rng([zlib.crc32(name.encode()), seed]).standard_normal(out[name].shape)
        drawn = base * np.exp(spread * noise) if base else spread * noise
        out[name] = jnp.asarray(drawn.astype(out[name].dtype))
    for name, factor in factors.items():
        out[name] = (out[name] * factor).astype(out[name].dtype)
    return out
```

```python
from contextlib import ExitStack

import numpy as np

import concourse.bass as bass
from concourse import mybir

F32 = mybir.dt.float32
F32R = mybir.dt.float32r
I32 = mybir.dt.int32
ALU = mybir.AluOpType
ACT = mybir.ActivationFunctionType

P = 128
S = 512
T = S // P
D = 1024
KD = D // P
DEPTH = 4
ALPHA = (2 * DEPTH) ** 0.25
LN_EPS = 1e-5
RMS_EPS = 1e-6
NEG = -1e30
BIG = 1e32
HD = 64
HEADS = 16
GROUP = 4
ROPE = 32
QH = HD + ROPE
QR, KVR = 384, 256
MLA_SCALE = float(QH) ** -0.5
SCALE = float(HD) ** -0.5
D_FF = 2816
KF = D_FF // P
KF_A = 16
TOPK = min(256, S // 4)
IDX_HEADS = 8
IDX_SCALE = (IDX_HEADS ** -0.5) * (64 ** -0.5)
TAKEN = -3e38
REL_L = 640
BUCKETS = 32

RING = 4
RAW = 3
LEAD = 3
UNIT = 1024

CAUSAL_KEYS = [128, 256, 384, 512]
WINDOW_KEYS = [128, 256, 256, 256]


def reads(src, c0, c1):
    return src[:, c0:c1].rearrange("(k p) n -> p k n", p=P)


def plan_units(w):
    units = []

    def tile(name, src, c0, n=P):
        units.append((name, KD, n, [(None, 0, n, reads(src, c0, c0 + n))], 0))

    def values(src, c0):
        for half in range(2):
            units.append(("v", KD // 2, 256, [(None, 0, 256, reads(src[half * 512:(half + 1) * 512, :], c0, c0 + 256))], 0))

    def rows(name, src, n, first=0):
        for k in range(first, first + n):
            units.append((name, 1, D, [(0, 0, D, src[k * P:(k + 1) * P, :])], 0))

    def mla(j):
        w_in, wq, wkv = w["mla_w_in"][j], w["mla_w_q_up"][j], w["mla_w_kv_up"][j]
        for i in range(5):
            tile("c", w_in, i * P)
        units.append(("krope", KD, P, [(None, 0, QH, reads(w_in, QR + KVR - HD, QR + KVR + ROPE))], 1))
        for i in range(KD):
            tile("gate", w_in, QR + KVR + ROPE + i * P)
        for g in range(HEADS // GROUP):
            for pair in range(2):
                h = GROUP * g + 2 * pair
                units.append(("q_up", QR // P, 2 * P,
                              [(None, i * P, QH, reads(wq, (h + i) * QH, (h + i + 1) * QH)) for i in range(2)], 1))
            loads = []
            for k in range(KVR // P):
                src = wkv[k * P:(k + 1) * P, g * 512:(g + 1) * 512].rearrange("p (h c) -> p h c", c=2 * HD)
                loads += [(k, 0, 256, src[:, :, 0:HD]), (k, 256, 256, src[:, :, HD:2 * HD])]
            units.append(("kv_up", KVR // P, 512, loads, 0))
        rows("out", w["mla_w_out"][j], KD)

    mla(0)
    swa = w["swa_w_in"][0]
    for i in range(2):
        tile("k", swa, D + i * P)
    values(swa, D + 256)
    for g in range(4):
        for i in range(2):
            tile("q", swa, (2 * g + i) * P)
        for i in range(2):
            tile("gate", swa, D + 512 + (2 * g + i) * P)
    rows("out", w["swa_w_out"][0], KD)
    fox = w["fox_w_in"][0]
    tile("f", fox, 3 * D, HEADS)
    for g in range(4):
        for i in range(2):
            tile("q", fox, (2 * g + i) * P)
        for i in range(2):
            tile("k", fox, D + (2 * g + i) * P)
        values(fox, 2 * D + 256 * g)
        for i in range(2):
            tile("gate", fox, 3 * D + HEADS + (2 * g + i) * P)
    rows("out", w["fox_w_out"][0], KD)
    mla(1)

    w_in = w["w_in_2"][0]
    cq, iq, ik, iw, dq = 1024, 1792, 2304, 2368, 2376
    ikv = reads(w_in, ik, ik + HD)
    units.append(("ik", KD, P, [(None, 0, HD, ikv), (None, HD, HD, ikv)], 0))
    tile("iw", w_in, iw, IDX_HEADS)
    for i in range(4):
        tile("iq", w_in, iq + i * P)
    for c in range(2):
        for part in range(3):
            tile("conv", w_in, 256 * part + c * P)
    for c in range(2):
        tile("pool", w_in, 768 + c * P)
    for base in (dq, cq):
        for i in range(2):
            tile("q", w_in, base + i * P)
        for i in range(2):
            tile("k", w_in, base + 256 + i * P)
        values(w_in, base + 512)
    rows("out", w["w_out_2"][0], KD)
    for lo, hi in ((0, KF_A), (KF_A, KF)):
        for m in range(lo, hi):
            tile("ff_gate", w["w_gate_up_2"][0], m * P)
            tile("ff_up", w["w_gate_up_2"][0], D_FF + m * P)
        rows("down", w["w_down_2"][0], hi - lo, lo)
    rows("ple_gate", w["w_ple_gate_2"][0], KD)
    rows("ple_proj", w["w_ple_proj_2"][0], 2)
    return units


def build(nc, w, consts, out):
    units = plan_units(w)
    ctx = ExitStack()
    with ctx:
        def sb(name, shape, dt=F32):
            return ctx.enter_context(nc.sbuf_tensor(name, shape, dt))

        def sem(name):
            return ctx.enter_context(nc.semaphore(name))

        XTh, XTl = sb("XTh", [P, KD, S], F32R), sb("XTl", [P, KD, S], F32R)
        OTh, OTl = sb("OTh", [P, KD, S], F32R), sb("OTl", [P, KD, S], F32R)
        QKh, QKl = sb("QKh", [P, 8, S], F32R), sb("QKl", [P, 8, S], F32R)
        x_tok = sb("x_tok", [P, T, D])
        V = sb("V", [P, T, 256])
        G = sb("G", [P, 8, S])
        PB = sb("PB", [P, 4096])
        misc = sb("misc", [P, 1152])
        w_raw = sb("w_raw", [P, RAW, UNIT])
        w_hi, w_lo = sb("w_hi", [P, RING, UNIT], F32R), sb("w_lo", [P, RING, UNIT], F32R)
        ident = sb("ident", [P, P])
        zmask = sb("zmask", [P, S])
        ones = sb("ones", [P, P])
        otmp = sb("otmp", [P, S])
        mx, nb, rs, es, ri = (sb(n, [P, 2, 4]) for n in ("mx", "nb", "rs", "es", "ri"))
        sink, nsink = sb("sink", [P, HEADS]), sb("nsink", [P, HEADS])
        qg = sb("qg", [P, 2, 5])
        bf = sb("bf", [HEADS, 1])
        st = sb("st", [P, 2, 6])
        mv = sb("mv", [P, 2])
        nv, ns, nt, rstd = (sb(n, [P, 1]) for n in ("nv", "ns", "nt", "rstd"))
        ssx, ssy = sb("ssx", [P, 2]), sb("ssy", [P, 2])
        iw_t = sb("iw_t", [P, T - 1, IDX_HEADS])
        top8 = sb("top8", [P, 8])
        conv_w = sb("conv_w", [P, 2, 3])
        pool_s = sb("pool_s", [P, 2])
        rel_t = sb("rel_t", [BUCKETS + 1, 8])
        scratch = nc.dram_tensor("rel_scratch", [8, P, REL_L], F32, kind="Internal").ap()
        bank = [ctx.enter_context(nc.psum_tensor(f"bank{i}", [P, S], F32)) for i in range(8)]
        S_BANK = [0, 1, 0, 2]
        S_COL = [0, 0, 128, 0]
        PT_BANK = [3, 4, 5, 4]
        PT_COL = [0, 0, 0, 384]
        PROJ = 6
        SB = [PB[:, 0:1280], PB[:, 1280:2560]]
        PT = PB[:, 2560:3840]
        vec = [PB[:, 0:1024], PB[:, 1024:2048]]
        YT = PB[:, 2048:3072]
        HT = PB[:, 3072:4096]

        raw_in = [sem(f"raw_in{i}") for i in range(RAW)]
        fixed = sem("fixed")
        hi_done = sem("hi_done")
        lo_done = sem("lo_done")
        w_mid = sem("w_mid")
        grp = sem("grp")
        bank_free = [sem("bank_free0"), sem("bank_free1")]
        g_hi = sem("g_hi")
        g_tmp = sem("g_tmp")
        s_done = sem("s_done")
        s_free = sem("s_free")
        nb_done = sem("nb_done")
        exp_done = sem("exp_done")
        p_done = sem("p_done")
        t_done = sem("t_done")
        t_free = sem("t_free")
        y_done = sem("y_done")
        y_sq = sem("y_sq")
        y_sum = sem("y_sum")
        y3 = sem("y3")
        x_new = sem("x_new")
        x_sq = sem("x_sq")
        src_done = sem("src_done")
        xt_done = sem("xt_done")
        xt_hi, xt_lo = sem("xt_hi"), sem("xt_lo")
        x_in = sem("x_in")
        cst, pool_cst = sem("cst"), sem("pool_cst")
        vec_in = [sem(f"vec_in{i}") for i in range(6)]
        rope_in, win_in, tri_in, pool_in, p_in, rel_in, onehot_in, rel_dma, aug_in = (
            sem(n) for n in ("rope_in", "win_in", "tri_in", "pool_in", "p_in", "rel_in", "onehot_in", "rel_dma", "aug_in"))
        own = sem("own")
        chain = sem("chain")
        sq_done = sem("sq_done")
        c_tmp, c_hi, c_lo = sem("c_tmp"), sem("c_hi"), sem("c_lo")
        kr_done = sem("kr_done")
        fx, fx_m = sem("fx"), sem("fx_m")
        idx_s, idx_r, idx_f = sem("idx_s"), sem("idx_r"), sem("idx_f")
        pool_r, pool_d = sem("pool_r"), sem("pool_d")
        ple_sg = sem("ple_sg")
        fin = sem("fin")
        out_done = sem("out_done")

        block = ctx.enter_context(nc.Block())

        class Count:
            def __init__(self):
                self.u = 0
                self.g = 0
                self.hi = 0
                self.tmp = 0
                self.head = 0
                self.tile = 0
                self.xt = 0
                self.src = 0
                self.own = 0
                self.cp = self.sq = self.vec = self.idx = self.aug = self.sg = 0
                self.misc = self.lat = self.lat_hi = self.lat_sq = 0

        gone = []
        mark = {}
        slot_at, raw_at, fix_at, n_fix = [0] * RAW, [], [], 0
        for u, unit in enumerate(units):
            slot_at[u % RAW] += 16 * len(unit[3])
            raw_at.append(slot_at[u % RAW])
            n_fix += 2 * unit[4]
            fix_at.append(n_fix)

        def view(t, u, ring):
            _, nk, ncol, _, _ = units[u]
            return t[:, u % ring, 0:nk * ncol].rearrange("p (k n) -> p k n", k=nk)

        def groups_stored(eng, n):
            for b in range(2):
                if (n + 1 - b) // 2:
                    eng.wait_ge(bank_free[b], (n + 1 - b) // 2)

        class Head:
            def __init__(self, q, k, rows, v, keys, scale, bias, dst, gate=None, sink=None, sel=False, packed=0):
                self.q, self.k, self.rows, self.v, self.keys, self.scale = q, k, rows, v, keys, scale
                self.bias, self.dst, self.gate, self.sink, self.sel, self.p0 = bias, dst, gate, sink, sel, packed
                self.window = keys is WINDOW_KEYS
                self.at = [sum(keys[:t]) for t in range(T)]
                self.pn = [256, 256, 256, 128] if self.window else [512, 384, 256, 128]
                self.pt = [0, self.pn[0], self.pn[0] + self.pn[1] + 128, self.pn[0] + self.pn[1]]

            def score(self, b, t):
                return SB[b][:, self.at[t]:self.at[t] + self.keys[t]]

            def tiles(self, j):
                return range(j, min(j + 2, T) if self.window else T)

        def causal(h):
            return lambda t: zmask[:, S - CAUSAL_KEYS[t]:S]

        def mla_heads(g):
            return [Head(i, 4 + i, QH, i * HD, CAUSAL_KEYS, MLA_SCALE, causal(i),
                         (XTh, XTl, 2 * g + i // 2, HD * (i % 2)), gate=2 * g + i // 2) for i in range(GROUP)]

        def swa_heads(g):
            return [Head(i, 4 + g, HD, g * HD, WINDOW_KEYS, SCALE,
                         lambda t, i=i: misc[:, 256 + 256 * (i % 2) + (128 if t == 0 else 0):512 + 256 * (i % 2)],
                         (OTh, OTl, 2 * g + i // 2, HD * (i % 2)), gate=2 * g + i // 2, sink=GROUP * g + i)
                    for i in range(GROUP)]

        def fox_heads(g):
            return [Head(i, 4 + i, HD + 2, i * HD, CAUSAL_KEYS, SCALE, causal(i),
                         (OTh, OTl, 2 * g + i // 2, HD * (i % 2)), gate=2 * g + i // 2) for i in range(GROUP)]

        def rel_heads(kind):
            first = 0 if kind == "dsa" else 4
            return [Head(i, 4 + i, HD, i * HD, CAUSAL_KEYS, SCALE,
                         lambda t, h=first + i: G[:, h, S - CAUSAL_KEYS[t]:S],
                         (OTh, OTl, (4 if kind == "dsa" else 6) + i // 2, HD * (i % 2)), sel=kind == "dsa")
                    for i in range(GROUP)]

        SEL = [None, misc[:, 0:256], misc[:, 256:640], misc[:, 640:1152]]
        WORK = SEL
        RELU = [PB[:, 896:1408], PB[:, 1408:1920]]
        CONV_A, CONV_H, CONV_Y = PB[:, 1920:2432], PB[:, 2446:2960], PB[:, 2976:3488]
        POOL_B = [PB[:, 1920:2448], PB[:, 2448:2976], PB[:, 2976:3504]]
        POOL_W = [PB[:, 3840 + P * c:3840 + P * (c + 1)] for c in range(2)]
        FZ, FA, FE, FL = (PB[0:HEADS, S * i:S * (i + 1)] for i in range(4))
        FT = PB[:, 2048:2048 + T * HEADS].rearrange("p (t h) -> p t h", t=T)
        TRI = PB[:, 3584:4096]
        REL_1H, REL_V = PB[0:BUCKETS + 1, 3072:3712], PB[0:8, 2048:2688]
        RT1, RT2 = PB[HD:QH, 3072:3584], PB[HD:QH, 3584:4096]
        SG = [PB[:, 0:512], PB[:, 512:1024]]
        Y3 = V[:, :, :].rearrange("p a b -> p (a b)")
        V2 = V[:, :, :].rearrange("p (c a) b -> p c (a b)", c=2)
        LT = PB[:, 2560:3072]
        ff_dst = [(QKh, QKl, m) if m < 8 else (OTh, OTl, m - 8) for m in range(KF_A)]
        ff_dst += [(QKh, QKl, m) for m in range(KF - KF_A)]

        CONSTANTS = [(ident[:, :], consts["ident"]), (zmask[:, :], consts["zmask"]),
                     (sink[:, :], w["swa_sinks"][0].partition_broadcast(P)),
                     (bf[:, :], w["fox_b_f"]), (pool_s[:, :], w["pool_scale_2"]), (rel_t[0:BUCKETS, :], w["rel_bias_2"]),
                     (conv_w[:, :, :], w["conv_w_2"]), (qg[:, :, 0:3], w["mla_q_norm"]), (qg[:, :, 3:5], w["mla_kv_norm"])]
        N_CST = 16 * len(CONSTANTS)

        @block.tensor
        def _(pe):
            c = Count()

            def three(o, ah, al, bh, bl, first, last):
                nc.tensor.matmul(o, ah, bh, start=first, stop=False, skip_group_check=True)
                nc.tensor.matmul(o, ah, bl, start=False, stop=False, skip_group_check=True)
                return nc.tensor.matmul(o, al, bh, start=False, stop=last, skip_group_check=True)

            def unit(name):
                assert units[c.u][0] == name, (name, units[c.u][0])
                pe.wait_ge(lo_done, c.u + 1)
                h, l = view(w_hi, c.u, RING), view(w_lo, c.u, RING)
                c.u += 1
                return h, l

            def begin():
                if c.g >= 2:
                    pe.wait_ge(bank_free[c.g % 2], c.g // 2)
                return bank[PROJ + c.g % 2]

            def end(mm):
                mm.then_inc(grp, 1)
                c.g += 1

            def released():
                gone.append((grp, c.g))

            def tile(name, n0=0, src=(XTh, XTl)):
                h, l = unit(name)
                o = begin()
                nk, m = h.shape[1], h.shape[2]
                for k in range(nk):
                    mm = three(o[0:m, 0:S - n0], h[:, k, :], l[:, k, :], src[0][:, k, n0:S], src[1][:, k, n0:S],
                               k == 0, k == nk - 1)
                end(mm)
                released()

            def values():
                parts = [unit("v"), unit("v")]
                for half in range(2):
                    o = begin()
                    for t in (2 * half, 2 * half + 1):
                        ts = slice(t * P, (t + 1) * P)
                        for k in range(KD):
                            h, l = parts[k // 4]
                            mm = three(o[:, 256 * (t % 2):256 * (t % 2) + 256], XTh[:, k, ts], XTl[:, k, ts],
                                       h[:, k % 4, :], l[:, k % 4, :], k == 0, k == KD - 1)
                    end(mm)
                released()
                released()

            def attention(heads):
                groups_stored(pe, c.g)
                a0 = c.head

                def scores(i):
                    hd, a = heads[i], a0 + i
                    r = slice(hd.p0, hd.p0 + hd.rows)
                    for t in (0, 2, 1, 3):
                        if t != 2 and a:
                            pe.wait_ge(s_free, 3 * (a - 1) + S_BANK[t] + 1)
                        ts = slice(t * P, (t + 1) * P)
                        ks = slice((t + 1) * P - hd.keys[t], (t + 1) * P)
                        mm = three(bank[S_BANK[t]][:, S_COL[t]:S_COL[t] + hd.keys[t]],
                                   QKh[r, hd.q, ts], QKl[r, hd.q, ts], QKh[r, hd.k, ks], QKl[r, hd.k, ks], True, True)
                        if t:
                            mm.then_inc(s_done, 1)

                def turn(i):
                    hd, a = heads[i], a0 + i
                    pe.wait_ge(p_done, a + 1)
                    for j in (0, 1, 3, 2):
                        if j != 3 and a:
                            pe.wait_ge(t_free, 3 * (a - 1) + j + 1)
                        for t in hd.tiles(j):
                            col = hd.at[t] + j * P - ((t + 1) * P - hd.keys[t])
                            o = (hd.pn[1] if j == 3 else 0) + (t - j) * P
                            mm = nc.tensor.transpose(bank[PT_BANK[j]][:, o:o + P], SB[a % 2][:, col:col + P], ident[:, :])
                        if j != 1:
                            mm.then_inc(t_done, 1)

                def mix(i):
                    hd, a = heads[i], a0 + i
                    o = begin()
                    pe.wait_ge(t_free, 3 * a + 3)
                    for j in range(T):
                        mm = nc.tensor.matmul(o[0:HD, j * P:j * P + hd.pn[j]], V[:, j, hd.v:hd.v + HD],
                                              PT[:, hd.pt[j]:hd.pt[j] + hd.pn[j]], start=(j == 0), stop=(j == T - 1),
                                              skip_group_check=True)
                    end(mm)

                scores(0)
                for i in range(len(heads)):
                    if i + 1 < len(heads):
                        scores(i + 1)
                    turn(i)
                    if i:
                        mix(i - 1)
                mix(len(heads) - 1)
                c.head += len(heads)

            def out_rows(name, n, src, first=True, last=True, before=None):
                groups_stored(pe, c.g)
                for k in range(n):
                    h, l = unit(name)
                    for t in range(T):
                        if before and k == 0:
                            before(t)
                        for half in range(2):
                            ah, al = src(k, slice(t * P, (t + 1) * P))
                            hs = slice(half * S, (half + 1) * S)
                            mm = three(bank[2 * t + half][:, :], ah, al, h[:, 0, hs], l[:, 0, hs],
                                       k == 0 and (first or t == T - 1), last and k == n - 1)
                        if last and k == n - 1:
                            mm.then_inc(y_done, 1)
                            c.tile += 1
                    if last and k == n - 1:
                        gone.append((y_done, c.tile))
                    else:
                        mm.then_inc(w_mid, 1)
                        c.sq += 1
                        gone.append((w_mid, c.sq))

            def turn_x(src, ready=None):
                for t in range(T):
                    if ready is None:
                        pe.wait_ge(src_done, c.src + 1)
                    elif t == 0:
                        pe.wait_ge(*ready)
                    c.src += ready is None
                    for half in range(2):
                        for i in range(4):
                            ch = 4 * half + i
                            mm = nc.tensor.transpose(bank[2 * t + half][:, i * P:(i + 1) * P],
                                                     src(t)[:, ch * P:(ch + 1) * P], ident[:, :])
                        mm.then_inc(xt_done, 1)
                        c.xt += 1
                pe.wait_ge(xt_lo, c.xt)

            def of(*tiles):
                return lambda k, ts: (tiles[0][:, k, ts], tiles[1][:, k, ts])

            def mla(j):
                for i in range(5):
                    tile("c")
                tile("krope")
                for i, n in ((0, 3), (3, 2)):
                    o = begin()
                    pe.wait_ge(sq_done, 5 * j + i + n)
                    for k in range(n):
                        mm = nc.tensor.matmul(o[:, :], ones[:, :], PB[:, S * (i + k):S * (i + k + 1)],
                                              start=(k == 0), stop=(k == n - 1))
                    end(mm)
                for i in range(KD):
                    tile("gate")
                pe.wait_ge(c_lo, 5 * (j + 1))
                for g in range(HEADS // GROUP):
                    for pair in range(2):
                        h, l = unit("q_up")
                        for i in range(2):
                            o = begin()
                            for k in range(3):
                                mm = three(o[:, :], h[:, k, i * P:(i + 1) * P], l[:, k, i * P:(i + 1) * P],
                                           OTh[:, k, :], OTl[:, k, :], k == 0, k == 2)
                            end(mm)
                        released()
                    h, l = unit("kv_up")
                    for pair in range(2):
                        o = begin()
                        for k in range(2):
                            mm = three(o[:, :], h[:, k, pair * P:(pair + 1) * P], l[:, k, pair * P:(pair + 1) * P],
                                       OTh[:, 3 + k, :], OTl[:, 3 + k, :], k == 0, k == 1)
                        end(mm)
                    for half in range(2):
                        o = begin()
                        for t in (2 * half, 2 * half + 1):
                            ts = slice(t * P, (t + 1) * P)
                            for k in range(2):
                                mm = three(o[:, 256 * (t % 2):256 * (t % 2) + 256], OTh[:, 3 + k, ts], OTl[:, 3 + k, ts],
                                           h[:, k, 256:512], l[:, k, 256:512], k == 0, k == 1)
                        end(mm)
                    released()
                    if g == 0:
                        pe.wait_ge(kr_done, 6 * (j + 1))
                        mark[f"mla{j}"] = c.g
                    attention(mla_heads(g))
                mark[f"vec{3 * j}"], mark[f"units{3 * j}"] = c.g, c.u + LEAD + 1
                out_rows("out", KD, of(XTh, XTl))
                turn_x((lambda t: HT) if j else (lambda t: x_tok[:, t, :]))

            pe.wait_ge(cst, N_CST)
            pe.wait_ge(pool_cst, 2)
            turn_x(lambda t: x_tok[:, t, :], (x_in, 16))
            pe.wait_ge(onehot_in, 16)
            for n in range(2):
                o = begin()
                nn = 512 if n == 0 else REL_L - 512
                end(nc.tensor.matmul(o[0:8, 0:nn], rel_t[:, :], REL_1H[:, n * 512:n * 512 + nn], start=True, stop=True))
            mark["rel"], mark["units_rel"] = c.g, LEAD
            mla(0)
            for i in range(2):
                tile("k")
            values()
            for g in range(4):
                for i in range(2):
                    tile("q")
                for i in range(2):
                    tile("gate")
                attention(swa_heads(g))
            mark["vec1"], mark["units1"] = c.g, c.u
            out_rows("out", KD, of(OTh, OTl))
            turn_x(lambda t: x_tok[:, t, :])
            tile("f")
            o = begin()
            pe.wait_ge(fx, 1)
            for t in range(T):
                mm = nc.tensor.transpose(o[:, HEADS * t:HEADS * (t + 1)], FL[:, t * P:(t + 1) * P], ident[0:HEADS, 0:HEADS])
            end(mm)
            o = begin()
            groups_stored(pe, c.g)
            pe.wait_ge(tri_in, 16)
            for t in range(T):
                mm = nc.tensor.matmul(o[0:HEADS, t * P:S], FT[:, t, :], TRI[:, 0:S - t * P], start=(t == 0), stop=(t == T - 1),
                                      skip_group_check=True)
            end(mm)
            mark["cum"] = c.g
            for g in range(4):
                for i in range(2):
                    tile("q")
                for i in range(2):
                    tile("k")
                values()
                for i in range(2):
                    tile("gate")
                pe.wait_ge(aug_in, 16 * (4 * (g + 1) + 4))
                mark[f"fox{g}"] = c.head
                attention(fox_heads(g))
            mark["vec2"], mark["units2"] = c.g, c.u + LEAD + 1
            out_rows("out", KD, of(OTh, OTl))
            turn_x(lambda t: x_tok[:, t, :])
            mla(1)
            tile("ik")
            h, l = unit("iw")
            o = begin()
            for t in range(1, T):
                for k in range(KD):
                    ts = slice(t * P, (t + 1) * P)
                    mm = three(o[:, IDX_HEADS * (t - 1):IDX_HEADS * t], XTh[:, k, ts], XTl[:, k, ts],
                               h[:, k, :], l[:, k, :], k == 0, k == KD - 1)
            end(mm)
            released()
            for i in range(4):
                tile("iq", n0=P)
            groups_stored(pe, c.g)
            for t in range(1, T):
                for h in range(IDX_HEADS):
                    n = c.idx
                    if n >= 2:
                        pe.wait_ge(idx_r, n - 1)
                    r = slice(HD * (h % 2), HD * (h % 2) + HD)
                    qs = slice((t - 1) * P, t * P)
                    keys = CAUSAL_KEYS[t]
                    three(bank[n % 2][:, 0:keys], QKh[r, h // 2, qs], QKl[r, h // 2, qs],
                          QKh[r, 4, 0:keys], QKl[r, 4, 0:keys], True, True).then_inc(idx_s, 1)
                    c.idx += 1
            for cc in range(2):
                for part in range(3):
                    tile("conv")
            for cc in range(2):
                tile("pool")
                o = begin()
                pe.wait_ge(pool_d, cc + 1)
                if cc == 0:
                    pe.wait_ge(pool_in, 80)
                end(nc.tensor.matmul(o[:, :], POOL_W[cc], POOL_B[0][:, 16:528], start=True, stop=True))
            for kind in ("moba", "dsa"):
                for i in range(2):
                    tile("q")
                for i in range(2):
                    tile("k")
                values()
                attention(rel_heads(kind))
            mark["vec4"], mark["units4"] = c.g, c.u
            out_rows("out", KD, of(OTh, OTl))
            turn_x(lambda t: HT)
            for lo, hi in ((0, KF_A), (KF_A, KF)):
                for m in range(lo, hi):
                    tile("ff_gate")
                    tile("ff_up")
                if lo:
                    mark["vec5"], mark["units5"] = c.g, c.u
                out_rows("down", hi - lo, lambda k, ts: (ff_dst[lo + k][0][:, ff_dst[lo + k][2], ts],
                                                         ff_dst[lo + k][1][:, ff_dst[lo + k][2], ts]),
                         first=lo == 0, last=lo > 0)
                if lo == 0:
                    mark["y3"] = c.sq
                    pe.wait_ge(y3, 2)
            turn_x(lambda t: HT)
            for cc in range(2):
                o = begin()
                pe.wait_ge(p_in, 16)
                for t in range(T):
                    mm = nc.tensor.transpose(o[:, t * P:(t + 1) * P], misc[:, 256 * t + cc * P:256 * t + (cc + 1) * P], ident[:, :])
                end(mm)
            out_rows("ple_gate", KD, of(XTh, XTl))
            out_rows("ple_proj", 2, of(QKh, QKl), before=lambda t: pe.wait_ge(ple_sg, t + 1))

        NU = len(gone)

        @block.sync
        def _(sp):
            sp.dma_start(x_tok[:, :, :], w["x"][0].rearrange("(t p) d -> p t d", p=P)).then_inc(x_in, 16)
            for u in range(NU):
                if u >= RAW:
                    sp.wait_ge(lo_done, u - RAW + 1)
                for k, c0, n, src in units[u][3]:
                    dst = view(w_raw, u, RAW)
                    if k is None:
                        dst = dst[:, :, c0:c0 + n]
                    else:
                        dst = dst[:, k, c0:c0 + n]
                        if len(src.shape) == 3:
                            dst = dst.rearrange("p (h c) -> p h c", c=HD)
                    sp.dma_start(dst, src).then_inc(raw_in[u % RAW], 16)
            for t in range(T):
                sp.wait_ge(fin, t + 1)
                sp.dma_start(out[0, t * P:(t + 1) * P, :], x_tok[:, t, :]).then_inc(out_done, 16)
            sp.wait_ge(out_done, 16 * T)

        @block.scalar
        def _(act):
            c = Count()

            def split(u):
                if u >= NU:
                    return
                act.wait_ge(raw_in[u % RAW], raw_at[u])
                if units[u][4]:
                    act.wait_ge(fixed, fix_at[u])
                if u >= RING:
                    act.wait_ge(*gone[u - RING])
                nc.scalar.activation(view(w_hi, u, RING), view(w_raw, u, RAW), ACT.Copy).then_inc(hi_done, 1)

            def advance(n=1):
                for _ in range(n):
                    split(c.u + LEAD)
                    c.u += 1

            def group():
                act.wait_ge(grp, c.g + 1)
                c.g += 1
                return bank[PROJ + (c.g - 1) % 2]

            def stored(ins):
                ins.then_inc(bank_free[(c.g - 1) % 2], 1)

            def hi(dst, src, scale=1.0):
                nc.scalar.activation(dst, src, ACT.Copy, scale=scale).then_inc(g_hi, 1)
                c.hi += 1

            def pair(slot):
                o = group()
                hi(QKh[0:HD, slot, :], o[0:HD, :])
                hi(QKh[0:HD, slot + 1, :], o[HD:P, :])

            def rotary(o, slot, nope=True):
                if nope:
                    hi(QKh[0:HD, slot, :], o[0:HD, :])
                act.wait_ge(g_tmp, c.tmp + 1)
                c.tmp += 1
                hi(QKh[HD:QH, slot, :], RT1)

            def values(half):
                o = group()
                stored(nc.scalar.activation(V[:, 2 * half:2 * half + 2, :], o[:, :].rearrange("p (t n) -> p t n", t=2), ACT.Copy))

            def value_units():
                advance()
                for half in range(2):
                    values(half)
                advance()

            def gate(i):
                o = group()
                stored(nc.scalar.activation(G[:, i, :], o[:, :], ACT.Silu))

            def from_tmp(dst, src=None):
                act.wait_ge(g_tmp, c.tmp + 1)
                c.tmp += 1
                hi(dst, otmp[:, :] if src is None else src)

            def attention(heads):
                a0, g0 = c.head, c.g

                def exps(i):
                    hd, a = heads[i], a0 + i
                    b = a % 2
                    act.wait_ge(nb_done, a + 1)
                    for t in range(T):
                        sc = hd.score(b, t)
                        ins = nc.scalar.activation(sc, sc, ACT.Exp, bias=nb[:, b, t:t + 1], scale=hd.scale,
                                                   accum_out=rs[:, b, t:t + 1])
                    if hd.sink is not None:
                        ins = nc.scalar.activation(es[:, b, :], nb[:, b, :], ACT.Exp, bias=sink[:, hd.sink:hd.sink + 1])
                    ins.then_inc(exp_done, 1)

                def turned(i):
                    hd, a = heads[i], a0 + i
                    if i:
                        act.wait_ge(grp, g0 + i)
                    for n, j in enumerate((0, 1, 2)):
                        act.wait_ge(t_done, 3 * a + n + 1)
                        width = hd.pn[j] + (P if j == 1 else 0)
                        nc.scalar.activation(PT[:, hd.pt[j]:hd.pt[j] + width], bank[PT_BANK[j]][:, 0:width], ACT.Copy)\
                            .then_inc(t_free, 1)

                def store(i):
                    hd = heads[i]
                    h, l, ch, r0 = hd.dst
                    o = group()
                    if hd.gate is None:
                        hi(h[r0:r0 + HD, ch, :], o[0:HD, :])
                    else:
                        from_tmp(h[r0:r0 + HD, ch, :], otmp[r0:r0 + HD, :])

                exps(0)
                for i in range(len(heads)):
                    if i + 1 < len(heads):
                        exps(i + 1)
                    if i >= 2:
                        store(i - 2)
                    turned(i)
                store(len(heads) - 2)
                store(len(heads) - 1)
                c.head += len(heads)

            def turn_x(between=None):
                for t in range(T):
                    if between:
                        between(t)
                    ts = slice(t * P, (t + 1) * P)
                    for half in range(2):
                        act.wait_ge(xt_done, c.xt + 1)
                        c.xt += 1
                        nc.scalar.activation(XTh[:, 4 * half:4 * half + 4, ts],
                                             bank[2 * t + half][:, :].rearrange("p (k n) -> p k n", k=4), ACT.Copy)\
                            .then_inc(xt_hi, 1)

            last = []

            def squares(src, out_sum, sm, n):
                for half in range(2):
                    if last:
                        act.wait_ge(*last.pop())
                    ins = nc.scalar.activation(otmp[:, :], src[half], ACT.Square, accum_out=out_sum[:, half:half + 1])
                    if half:
                        ins.then_inc(sm, 1)
                        last.append((sm, n))
                    else:
                        ins.then_inc(own, 1)
                        c.own += 1
                        last.append((own, c.own))

            def x_squares(t):
                act.wait_ge(x_new, c.sq + 1)
                c.sq += 1
                squares([x_tok[:, t, 0:S], x_tok[:, t, S:D]], ssx, x_sq, c.sq)

            def rms_tail(last_saved=False):
                def between(t):
                    if last_saved and t == T - 1:
                        act.wait_ge(y_sum, 1)
                        src = [YT[:, 0:S], YT[:, S:D]]
                    else:
                        act.wait_ge(y_done, c.tile + 1)
                        src = [bank[2 * t][:, :], bank[2 * t + 1][:, :]]
                    c.tile += 1
                    c.cp += 1
                    squares(src, ssy, y_sq, c.cp)
                    x_squares(t)
                turn_x(between)

            def mla(j):
                for i in range(5):
                    advance()
                    o = group()
                    nc.scalar.activation(PB[:, S * i:S * (i + 1)], o[:, :], ACT.Square).then_inc(sq_done, 1)
                    stored(nc.scalar.activation(G[:, i, :], o[:, :], ACT.Copy))
                advance()
                rotary(group(), 4, nope=False)
                for s in range(3):
                    if s == 0:
                        act.wait_ge(g_hi, c.hi)
                    nc.scalar.activation(QKh[HD:QH, 5 + s, :], QKh[HD:QH, 4, :].bitcast(F32), ACT.Copy).then_inc(kr_done, 1)
                c.g += 2
                for i in range(5):
                    act.wait_ge(c_tmp, 5 * j + i + 1)
                    nc.scalar.activation(OTh[:, i, :], G[:, i, :], ACT.Copy).then_inc(c_hi, 1)
                act.wait_ge(c_lo, 5 * (j + 1))
                for i in range(KD):
                    advance()
                    gate(i)
                for g in range(HEADS // GROUP):
                    for p2 in range(2):
                        advance()
                        for i in range(2):
                            rotary(group(), 2 * p2 + i)
                    advance()
                    for p2 in range(2):
                        pair(4 + 2 * p2)
                    for half in range(2):
                        values(half)
                    attention(mla_heads(g))
                advance(KD)
                c.tile += T
                turn_x(x_squares if j else None)

            for u in range(LEAD):
                split(u)
            turn_x()
            for n in range(2):
                o = group()
                nn = 512 if n == 0 else REL_L - 512
                stored(nc.scalar.activation(REL_V[:, n * 512:n * 512 + nn], o[0:8, 0:nn], ACT.Copy, scale=1.0 / SCALE))
            act.wait_ge(rel_dma, 16)
            mla(0)
            for i in range(2):
                advance()
                pair(4 + 2 * i)
            value_units()
            for g in range(4):
                for i in range(2):
                    advance()
                    pair(2 * i)
                for i in range(2):
                    advance()
                    gate(2 * g + i)
                attention(swa_heads(g))
            advance(KD)
            c.tile += T
            turn_x()
            advance()
            o = group()
            act.wait_ge(cst, N_CST)
            stored(nc.scalar.activation(FZ, o[0:HEADS, :], ACT.Identity, bias=bf[:, 0:1]))
            groups_stored(act, c.g)
            nc.scalar.activation(FA, FZ, ACT.Abs).then_inc(own, 1)
            act.wait_ge(own, 1)
            nc.scalar.activation(FE, FA, ACT.Exp, scale=-1.0).then_inc(own, 1)
            act.wait_ge(own, 2)
            nc.scalar.activation(FA, FE, ACT.Ln, bias=1.0).then_inc(own, 1)
            c.own = 3
            o = group()
            stored(nc.scalar.activation(FT, o[:, 0:T * HEADS].rearrange("p (t h) -> p t h", t=T), ACT.Copy))
            o = group()
            hi(OTh[0:HEADS, 7, :], o[0:HEADS, :], scale=1.0 / SCALE)
            hi(OTh[0:HEADS, 6, :], o[0:HEADS, :], scale=-1.0 / SCALE)
            for g in range(4):
                for i in range(2):
                    advance()
                    pair(2 * i)
                for i in range(2):
                    advance()
                    pair(4 + 2 * i)
                value_units()
                for i in range(2):
                    advance()
                    gate(2 * g + i)
                attention(fox_heads(g))
            advance(KD)
            c.tile += T
            turn_x()
            mla(1)
            advance()
            hi(QKh[:, 4, :], group()[:, :])
            advance()
            stored(nc.scalar.activation(iw_t[:, :, :], group()[:, 0:3 * IDX_HEADS].rearrange("p (t h) -> p t h", t=3), ACT.Copy))
            for i in range(4):
                advance()
                hi(QKh[:, i, 0:S - P], group()[:, 0:S - P])
            for t in range(1, T):
                for h in range(IDX_HEADS):
                    n = c.idx
                    act.wait_ge(idx_s, n + 1)
                    if n >= 2:
                        act.wait_ge(idx_f, n - 1)
                    keys = CAUSAL_KEYS[t]
                    nc.scalar.activation(RELU[n % 2][:, 0:keys], bank[n % 2][:, 0:keys], ACT.Relu).then_inc(idx_r, 1)
                    c.idx += 1
            for cc in range(2):
                advance()
                stored(nc.scalar.activation(CONV_A, group()[:, :], ACT.Copy))
                advance()
                c.g += 1
                advance()
                c.g += 1
                from_tmp(OTh[:, cc, :])
            for cc in range(2):
                advance()
                o = group()
                act.wait_ge(pool_r, 1 + cc)
                stored(nc.scalar.activation(POOL_B[0][:, 16:528], o[:, :], ACT.Copy))
                c.g += 1
                from_tmp(OTh[:, 2 + cc, :])
            for kind in ("moba", "dsa"):
                for i in range(2):
                    advance()
                    pair(2 * i)
                for i in range(2):
                    advance()
                    pair(4 + 2 * i)
                value_units()
                attention(rel_heads(kind))
            advance(KD)
            rms_tail()
            for lo, hi_m in ((0, KF_A), (KF_A, KF)):
                for m in range(lo, hi_m):
                    advance()
                    stored(nc.scalar.activation(SG[m % 2], group()[:, :], ACT.Silu))
                    advance()
                    c.g += 1
                    h, l, ch = ff_dst[m]
                    from_tmp(h[:, ch, :])
                advance(hi_m - lo)
                if lo == 0:
                    act.wait_ge(w_mid, mark["y3"])
                    for half in range(2):
                        nc.scalar.activation(Y3[:, half * S:half * S + S], bank[6 + half][:, :], ACT.Copy).then_inc(y3, 1)
            rms_tail(last_saved=True)
            for cc in range(2):
                hi(QKh[:, cc, :], group()[:, :])
            advance(KD)
            for t in range(T):
                act.wait_ge(y_done, c.tile + 1)
                c.tile += 1
                for half in range(2):
                    ins = nc.scalar.activation(G[:, 2 * t + half, :], bank[2 * t + half][:, :], ACT.Sigmoid)
                ins.then_inc(ple_sg, 1)
            advance(2)

        @block.vector
        def _(dve):
            c = Count()

            def split(u):
                if u >= NU:
                    return
                dve.wait_ge(hi_done, u + 1)
                nc.vector.tensor_tensor(view(w_lo, u, RING), view(w_raw, u, RAW), view(w_hi, u, RING).bitcast(F32),
                                        ALU.subtract).then_inc(lo_done, 1)

            def advance(n=1):
                for _ in range(n):
                    split(c.u + LEAD)
                    c.u += 1

            def link(ins):
                ins.then_inc(chain, 1)
                c.own += 1
                dve.wait_ge(chain, c.own)

            def group():
                dve.wait_ge(grp, c.g + 1)
                c.g += 1
                return bank[PROJ + (c.g - 1) % 2]

            def stored(ins):
                ins.then_inc(bank_free[(c.g - 1) % 2], 1)

            def lo(dst, src, h):
                c.hi += 1
                dve.wait_ge(g_hi, c.hi)
                return nc.vector.tensor_tensor(dst, src, h.bitcast(F32), ALU.subtract)

            def pair(slot):
                o = group()
                lo(QKl[0:HD, slot, :], o[0:HD, :], QKh[0:HD, slot, :])
                stored(lo(QKl[0:HD, slot + 1, :], o[HD:P, :], QKh[0:HD, slot + 1, :]))

            def rotary(o, slot, nope=True):
                groups_stored(dve, c.g - 1)
                nc.vector.tensor_tensor(RT1, o[HD:QH, :], misc[HD:QH, 0:S], ALU.mult)
                link(nc.vector.tensor_tensor(RT2, o[QH:P, :], misc[QH:P, 0:S], ALU.mult))
                nc.vector.tensor_tensor(RT1, RT1, RT2, ALU.add).then_inc(g_tmp, 1)
                if nope:
                    lo(QKl[0:HD, slot, :], o[0:HD, :], QKh[0:HD, slot, :])
                stored(lo(QKl[HD:QH, slot, :], RT1, QKh[HD:QH, slot, :]))

            def root(v, r, s, t):
                link(nc.vector.tensor_scalar(r.bitcast(I32), v.bitcast(I32), -0.5, float(0x5f3759df), ALU.mult, ALU.add))
                x, y, f = r, s, 1.0
                for _ in range(3):
                    link(nc.vector.tensor_tensor(t, v, x, ALU.mult))
                    link(nc.vector.tensor_tensor(t, t, x, ALU.mult))
                    link(nc.vector.scalar_tensor_tensor(y, t, -3.0 * f * f, x, ALU.add, ALU.mult))
                    f = -2.0 * f ** 3
                    x, y = y, x
                link(nc.vector.tensor_scalar(r, x, 1.0 / f, None, ALU.mult))

            def attention(heads, between=None):
                a0, g0 = c.head, c.g

                def maxima(i):
                    hd, a = heads[i], a0 + i
                    b = a % 2
                    if a >= 2:
                        dve.wait_ge(t_done, 3 * (a - 1))
                    if hd.window:
                        slope = 2.0 ** (-8.0 * (hd.sink + 1) / HEADS)
                        link(nc.vector.tensor_scalar(misc[:, 256 + 256 * (i % 2):512 + 256 * (i % 2)], misc[:, 0:256],
                                                     -slope / hd.scale, None, ALU.mult))
                    for t in (0, 2, 1, 3):
                        dve.wait_ge(s_done, 3 * a + S_BANK[t] + 1)
                        o = bank[S_BANK[t]][:, S_COL[t]:S_COL[t] + hd.keys[t]]
                        if hd.sel and t:
                            link(nc.vector.tensor_tensor(hd.score(b, t), o, hd.bias(t), ALU.add))
                            ins = nc.vector.tensor_tensor_reduce(hd.score(b, t), hd.score(b, t), SEL[t], 1.0, -3e38,
                                                                 ALU.add, ALU.max, mx[:, b, t:t + 1])
                        else:
                            ins = nc.vector.tensor_tensor_reduce(hd.score(b, t), o, hd.bias(t), 1.0, -3e38,
                                                                 ALU.add, ALU.max, mx[:, b, t:t + 1])
                        if t:
                            ins.then_inc(s_free, 1)
                    dve.wait_ge(s_free, 3 * a + 3)
                    if hd.sink is None:
                        ins = nc.vector.tensor_scalar(nb[:, b, :], mx[:, b, :], -hd.scale, None, ALU.mult)
                    else:
                        ins = nc.vector.tensor_scalar(nb[:, b, :], mx[:, b, :], -hd.scale, nsink[:, hd.sink:hd.sink + 1],
                                                      ALU.mult, ALU.min)
                    ins.then_inc(nb_done, 1)

                def norm(i):
                    hd, a = heads[i], a0 + i
                    b = a % 2
                    dve.wait_ge(exp_done, a + 1)
                    if hd.sink is not None:
                        link(nc.vector.tensor_tensor(rs[:, b, :], rs[:, b, :], es[:, b, :], ALU.add))
                    link(nc.vector.reciprocal(ri[:, b, :], rs[:, b, :]))
                    for t in range(T):
                        ins = nc.vector.tensor_scalar(hd.score(b, t), hd.score(b, t), ri[:, b, t:t + 1], None, ALU.mult)
                    ins.then_inc(p_done, 1)

                def store(i):
                    hd = heads[i]
                    h, l, ch, r0 = hd.dst
                    o = group()
                    rows = slice(r0, r0 + HD)
                    groups_stored(dve, c.g - 1)
                    if hd.gate is None:
                        stored(lo(l[rows, ch, :], o[0:HD, :], h[rows, ch, :]))
                        return
                    nc.vector.tensor_tensor(otmp[rows, :], o[0:HD, :], G[rows, hd.gate, :], ALU.mult).then_inc(g_tmp, 1)
                    stored(lo(l[rows, ch, :], otmp[rows, :], h[rows, ch, :]))

                groups_stored(dve, c.g)
                maxima(0)
                for i in range(len(heads)):
                    norm(i)
                    if i + 1 < len(heads):
                        maxima(i + 1)
                    if i >= 2:
                        store(i - 2)
                    if between:
                        between()
                store(len(heads) - 2)
                store(len(heads) - 1)
                c.head += len(heads)

            def turn_x(make=None):
                def low(t):
                    ts = slice(t * P, (t + 1) * P)
                    for half in range(2):
                        dve.wait_ge(xt_hi, c.xt + 1)
                        c.xt += 1
                        ks = slice(4 * half, 4 * half + 4)
                        nc.vector.tensor_tensor(XTl[:, ks, ts], bank[2 * t + half][:, :].rearrange("p (k n) -> p k n", k=4),
                                                XTh[:, ks, ts].bitcast(F32), ALU.subtract).then_inc(xt_lo, 1)
                for t in range(T):
                    if make:
                        if t:
                            dve.wait_ge(src_done, c.src)
                        make(t)
                        c.src += 1
                        if t:
                            low(t - 1)
                    else:
                        low(t)
                if make:
                    low(T - 1)

            def rms_root(sums, sm, n):
                dve.wait_ge(sm, n)
                link(nc.vector.tensor_tensor(nv[:, :], sums[:, 0:1], sums[:, 1:2], ALU.add))
                link(nc.vector.tensor_scalar(nv[:, :], nv[:, :], 1.0 / D, RMS_EPS, ALU.mult, ALU.add))
                root(nv[:, :], rstd[:, :], ns[:, :], nt[:, :])

            def h_norm(t, gain):
                c.sq += 1
                rms_root(ssx, x_sq, c.sq)
                if t:
                    dve.wait_ge(xt_done, c.xt)
                nc.vector.scalar_tensor_tensor(HT, x_tok[:, t, :], rstd[:, 0:1], gain, ALU.mult, ALU.mult).then_inc(src_done, 1)

            def ln_tail(i):
                def make(t):
                    if t == 0:
                        dve.wait_ge(vec_in[i], 16 * (3 if i == 3 else 2))
                    dve.wait_ge(y_done, c.tile + 1)
                    c.tile += 1
                    for half in range(2):
                        hs = slice(half * S, half * S + S)
                        ins = nc.vector.scalar_tensor_tensor(YT[:, hs], x_tok[:, t, hs], ALPHA, bank[2 * t + half][:, :],
                                                             ALU.mult, ALU.add)
                    link(ins)
                    nc.vector.bn_stats(st[:, 0, :], YT[:, 0:S])
                    link(nc.vector.bn_stats(st[:, 1, :], YT[:, S:D]))
                    link(nc.vector.bn_aggr(mv[:, :], st[:, :, :].rearrange("p a b -> p (a b)")))
                    link(nc.vector.tensor_scalar(nv[:, :], mv[:, 1:2], LN_EPS, None, ALU.add))
                    root(nv[:, :], rstd[:, :], ns[:, :], nt[:, :])
                    link(nc.vector.scalar_tensor_tensor(YT, YT, mv[:, 0:1], vec[0], ALU.subtract, ALU.mult))
                    ins = nc.vector.scalar_tensor_tensor(x_tok[:, t, :], YT, rstd[:, 0:1], vec[1], ALU.mult, ALU.add)
                    if i == 3:
                        ins.then_inc(x_new, 1)
                        dve.wait_ge(x_new, t + 1)
                        h_norm(t, V[:, :, :].rearrange("p a b -> p (a b)"))
                    else:
                        ins.then_inc(src_done, 1)
                turn_x(make)

            def rms_tail(n, last_saved=False):
                def make(t):
                    if t == 0:
                        dve.wait_ge(vec_in[n], 32)
                    src = [bank[2 * t], bank[2 * t + 1]]
                    c.tile += 1
                    if last_saved and t == T - 1:
                        dve.wait_ge(y_done, c.tile)
                        for half in range(2):
                            hs = slice(half * S, half * S + S)
                            ins = nc.vector.tensor_tensor(YT[:, hs], bank[2 * t + half][:, :], Y3[:, hs], ALU.add)
                        ins.then_inc(y_sum, 1)
                        src = [YT[:, 0:S], YT[:, S:D]]
                    c.cp += 1
                    rms_root(ssy, y_sq, c.cp)
                    for half in range(2):
                        hs = slice(half * S, half * S + S)
                        ins = nc.vector.scalar_tensor_tensor(YT[:, hs], src[half][:, :], rstd[:, 0:1], vec[0][:, hs],
                                                             ALU.mult, ALU.mult)
                    link(ins)
                    nc.vector.tensor_tensor(x_tok[:, t, :], x_tok[:, t, :], YT, ALU.add).then_inc(x_new, 1)
                    h_norm(t, vec[1])
                turn_x(make)

            def mla(j):
                advance(5)
                c.g += 5
                advance()
                dve.wait_ge(rope_in, 16 * (j + 1))
                rotary(group(), 4, nope=False)
                groups_stored(dve, c.g)
                for s in range(3):
                    nc.vector.tensor_copy(QKl[HD:QH, 5 + s, :], QKl[HD:QH, 4, :].bitcast(F32)).then_inc(kr_done, 1)
                for i0, n in ((0, 3), (3, 2)):
                    o = group()
                    stored(nc.vector.tensor_scalar(G[:, 5, :], o[:, :], 1.0 / (n * P), RMS_EPS, ALU.mult, ALU.add))
                    groups_stored(dve, c.g)
                    root(G[:, 5, :], LT, G[:, 6, :], G[:, 7, :])
                    for i in range(i0, i0 + n):
                        nc.vector.scalar_tensor_tensor(G[:, i, :], G[:, i, :], qg[:, j, i:i + 1], LT, ALU.mult, ALU.mult)\
                            .then_inc(c_tmp, 1)
                for i in range(5):
                    dve.wait_ge(c_hi, 5 * j + i + 1)
                    nc.vector.tensor_tensor(OTl[:, i, :], G[:, i, :], OTh[:, i, :].bitcast(F32), ALU.subtract).then_inc(c_lo, 1)
                advance(KD)
                c.g += KD
                for g in range(HEADS // GROUP):
                    for p2 in range(2):
                        advance()
                        for i in range(2):
                            rotary(group(), 2 * p2 + i)
                    advance()
                    for p2 in range(2):
                        pair(4 + 2 * p2)
                    c.g += 2
                    attention(mla_heads(g))
                advance(KD)
                ln_tail(3 * j)

            dve.wait_ge(cst, N_CST)
            for u in range(LEAD):
                split(u)
            nc.vector.tensor_scalar(nsink[:, :], sink[:, :], -1.0, None, ALU.mult)
            turn_x()
            c.g += 2
            mla(0)
            for i in range(2):
                advance()
                pair(4 + 2 * i)
            advance(2)
            c.g += 2
            dve.wait_ge(win_in, 16)
            for g in range(4):
                for i in range(2):
                    advance()
                    pair(2 * i)
                advance(2)
                c.g += 2
                attention(swa_heads(g))
            advance(KD)
            ln_tail(1)
            advance()
            c.g += 1
            nc.vector.memset(OTh[32:64, 7, :].bitcast(F32), 1.0).then_inc(fx_m, 1)
            nc.vector.memset(OTl[32:64, 7, :].bitcast(F32), 0.0).then_inc(fx_m, 1)
            dve.wait_ge(own, 3)
            nc.vector.scalar_tensor_tensor(FL, FZ, 0.0, FA, ALU.min, ALU.subtract).then_inc(fx, 1)
            c.g += 1
            o = group()
            c.hi += 2
            dve.wait_ge(g_hi, c.hi)
            for ch, s in ((7, 1.0 / SCALE), (6, -1.0 / SCALE)):
                ins = nc.vector.scalar_tensor_tensor(OTl[0:HEADS, ch, :], o[0:HEADS, :], s, OTh[0:HEADS, ch, :].bitcast(F32),
                                                     ALU.mult, ALU.subtract)
            stored(ins)
            for g in range(4):
                for i in range(2):
                    advance()
                    pair(2 * i)
                for i in range(2):
                    advance()
                    pair(4 + 2 * i)
                advance(4)
                c.g += 4
                attention(fox_heads(g))
            advance(KD)
            ln_tail(2)
            mla(1)
            advance()
            o = group()
            stored(lo(QKl[:, 4, :], o[:, :], QKh[:, 4, :]))
            advance()
            c.g += 1
            for i in range(4):
                advance()
                o = group()
                stored(lo(QKl[:, i, 0:S - P], o[:, 0:S - P], QKh[:, i, 0:S - P]))
            groups_stored(dve, c.g)
            for t in range(1, T):
                for h in range(IDX_HEADS):
                    n = c.idx
                    dve.wait_ge(idx_r, n + 1)
                    r = RELU[n % 2][:, 0:CAUSAL_KEYS[t]]
                    if h == 0:
                        ins = nc.vector.tensor_scalar(WORK[t], r, iw_t[:, t - 1, h:h + 1], None, ALU.mult)
                    else:
                        dve.wait_ge(idx_f, n)
                        ins = nc.vector.scalar_tensor_tensor(WORK[t], r, iw_t[:, t - 1, h:h + 1], WORK[t], ALU.mult, ALU.add)
                    ins.then_inc(idx_f, 1)
                    c.idx += 1
                dve.wait_ge(idx_f, c.idx)
                link(nc.vector.scalar_tensor_tensor(WORK[t], WORK[t], IDX_SCALE, zmask[:, S - CAUSAL_KEYS[t]:S],
                                                    ALU.mult, ALU.add))
            rounds = [t for t in range(1, T) for _ in range(TOPK // 8)]

            def top(n):
                for _ in range(min(n, len(rounds))):
                    t = rounds.pop(0)
                    link(nc.vector.max(top8[:, :], WORK[t]))
                    link(nc.vector.match_replace(WORK[t], top8[:, :], WORK[t], TAKEN))

            nc.vector.memset(PB[:, 2446:2448], 0.0)
            for cc in range(2):
                advance()
                c.g += 1
                top(2)
                advance()
                o = group()
                groups_stored(dve, c.g - 1)
                stored(nc.vector.tensor_tensor(CONV_H[:, 2:514], o[:, :], CONV_A, ALU.mult))
                groups_stored(dve, c.g)
                link(nc.vector.tensor_scalar(CONV_Y, CONV_H[:, 0:512], conv_w[:, cc, 0:1], None, ALU.mult))
                for tap in (1, 2):
                    link(nc.vector.scalar_tensor_tensor(CONV_Y, CONV_H[:, tap:tap + 512], conv_w[:, cc, tap:tap + 1], CONV_Y,
                                                        ALU.mult, ALU.add))
                advance()
                o = group()
                groups_stored(dve, c.g - 1)
                nc.vector.tensor_tensor(otmp[:, :], o[:, :], CONV_Y, ALU.mult).then_inc(g_tmp, 1)
                stored(lo(OTl[:, cc, :], otmp[:, :], OTh[:, cc, :]))
            for b in range(3):
                ins = nc.vector.memset(POOL_B[b][:, 0:16], 0.0)
            ins.then_inc(pool_r, 1)
            dve.wait_ge(pool_in, 80)
            for cc in range(2):
                advance()
                c.g += 1
                groups_stored(dve, c.g)
                v0, b1, b2 = POOL_B

                def doubled(dst, src, by):
                    link(nc.vector.tensor_tensor(dst[:, 16:528], src[:, 16:528], src[:, 16 - by:528 - by], ALU.add))

                doubled(b1, v0, 1)
                doubled(b2, b1, 2)
                if cc:
                    doubled(b1, b2, 4)
                    doubled(b2, b1, 8)
                for b, rows in ((b1, slice(0, HD)), (b2, slice(HD, P))):
                    link(nc.vector.tensor_tensor(b[rows, 16:528], b[rows, 16:528], V2[rows, cc, :], ALU.mult))
                    ins = nc.vector.tensor_tensor(v0[rows, 16:528], b[rows, 16:528], v0[rows, 16:528], ALU.subtract)
                ins.then_inc(pool_d, 1)
                o = group()
                groups_stored(dve, c.g - 1)
                if cc:
                    nc.vector.tensor_scalar(otmp[:, :], o[:, :], pool_s[:, cc:cc + 1], None, ALU.mult).then_inc(g_tmp, 1)
                else:
                    nc.vector.tensor_scalar(otmp[:, :], o[:, :], pool_s[:, cc:cc + 1], None, ALU.mult).then_inc(g_tmp, 1)
                    nc.vector.memset(POOL_B[0][:, 0:16], 0.0).then_inc(pool_r, 1)
                stored(lo(OTl[:, 2 + cc, :], otmp[:, :], OTh[:, 2 + cc, :]))
                top(2)
            dve.wait_ge(rel_in, 16 * 8)
            for kind in ("moba", "dsa"):
                for i in range(2):
                    advance()
                    pair(2 * i)
                    top(3)
                for i in range(2):
                    advance()
                    pair(4 + 2 * i)
                    top(3)
                advance(2)
                c.g += 2
                if kind == "dsa":
                    top(64)
                    link(nc.vector.tensor_scalar(misc[:, :], misc[:, :], TAKEN / 2, NEG, ALU.is_gt, ALU.mult))
                attention(rel_heads(kind), between=lambda: top(2))
            advance(KD)
            rms_tail(4)
            for lo_m, hi_m in ((0, KF_A), (KF_A, KF)):
                for m in range(lo_m, hi_m):
                    advance()
                    c.g += 1
                    advance()
                    o = group()
                    groups_stored(dve, c.g - 1)
                    h, l, ch = ff_dst[m]
                    nc.vector.tensor_tensor(otmp[:, :], o[:, :], SG[m % 2], ALU.mult).then_inc(g_tmp, 1)
                    stored(lo(l[:, ch, :], otmp[:, :], h[:, ch, :]))
                advance(hi_m - lo_m)
            dve.wait_ge(y3, 2)
            rms_tail(5, last_saved=True)
            for cc in range(2):
                o = group()
                stored(lo(QKl[:, cc, :], o[:, :], QKh[:, cc, :]))
            advance(KD)
            c.tile += T
            advance(2)
            for t in range(T):
                dve.wait_ge(ple_sg, t + 1)
                if t:
                    dve.wait_ge(fin, t)
                dve.wait_ge(y_done, c.tile + 1)
                c.tile += 1
                for half in range(2):
                    hs = slice(half * S, half * S + S)
                    ins = nc.vector.tensor_tensor(YT[:, hs], bank[2 * t + half][:, :], G[:, 2 * t + half, :], ALU.mult)
                link(ins)
                nc.vector.tensor_tensor(x_tok[:, t, :], x_tok[:, t, :], YT, ALU.add).then_inc(fin, 1)

        @block.gpsimd
        def _(pool):
            done = [0]

            for dst, src in CONSTANTS:
                pool.dma_start(dst, src).then_inc(cst, 16)
            pool.memset(ones[:, :], 1.0).then_inc(pool_cst, 1)
            pool.wait_ge(pool_cst, 1)
            pool.memset(rel_t[BUCKETS:BUCKETS + 1, :], 1.0).then_inc(pool_cst, 1)
            pool.dma_start(REL_1H, consts["onehot"]).then_inc(onehot_in, 16)
            pool.dma_start(misc[HD:P, 0:S], consts["rope"]).then_inc(rope_in, 16)

            def fixups(name):
                while done[0] < min(mark[name], NU):
                    u = done[0]
                    done[0] += 1
                    if units[u][4]:
                        _, nk, ncol, _, _ = units[u]
                        pool.wait_ge(raw_in[u % RAW], raw_at[u])
                        v = w_raw[:, u % RAW, 0:nk * ncol].rearrange("p (a n) -> p a n", n=P)
                        pool.tensor_copy(v[:, :, QH:QH + 16], v[:, :, HD + 16:QH]).then_inc(fixed, 1)
                        pool.tensor_copy(v[:, :, QH + 16:P], v[:, :, HD:HD + 16]).then_inc(fixed, 1)

            def vectors(i, *names):
                fixups(f"units{i}")
                groups_stored(pool, mark[f"vec{i}"])
                for n, v in enumerate(names):
                    dst = vec[n] if n < 2 else V[:, :, :].rearrange("p a b -> p (a b)")
                    pool.dma_start(dst, v.partition_broadcast(P)).then_inc(vec_in[i], 16)

            def turned(n):
                pool.wait_ge(xt_lo, 2 * T * n)

            fixups("units_rel")
            groups_stored(pool, mark["rel"])
            pool.dma_start(scratch, REL_V[:, None, 0:REL_L].to_broadcast([8, P, REL_L])).then_inc(rel_dma, 16)
            vectors(0, w["ln_g"][0], w["ln_b"][0])
            turned(2)
            pool.dma_start(misc[:, 0:256], consts["window"]).then_inc(win_in, 16)
            vectors(1, w["ln_g"][1], w["ln_b"][1])
            turned(3)
            pool.dma_start(misc[HD:P, 0:S], consts["rope"]).then_inc(rope_in, 16)
            pool.dma_start(TRI, consts["tri"]).then_inc(tri_in, 16)
            groups_stored(pool, mark["cum"])
            pool.wait_ge(fx_m, 2)
            for g in range(4):
                hs = slice(GROUP * g, GROUP * g + GROUP)
                if g:
                    pool.wait_ge(s_done, 3 * (mark[f"fox{g}"]))
                for dst, src in ((QKh[64:65, 0:4, :], OTh[hs, 7, :]), (QKl[64:65, 0:4, :], OTl[hs, 7, :]),
                                 (QKh[65:66, 4:8, :], OTh[hs, 6, :]), (QKl[65:66, 4:8, :], OTl[hs, 6, :])):
                    pool.dma_start(dst, src).then_inc(aug_in, 16)
                if g == 0:
                    for dst, src in ((QKh, OTh[32:36, 7, :]), (QKl, OTl[32:36, 7, :])):
                        pool.dma_start(dst[65:66, 0:4, :], src).then_inc(aug_in, 16)
                        pool.dma_start(dst[64:65, 4:8, :], src).then_inc(aug_in, 16)
            vectors(2, w["ln_g"][2], w["ln_b"][2])
            vectors(3, w["ln_g"][3], w["ln_b"][3], w["g_mix_pre_2"][0])
            turned(5)
            pool.dma_start(V2, consts["counts"]).then_inc(pool_in, 16)
            pool.memset(PB[:, 3840:4096], 0.0).then_inc(pool_cst, 1)
            pool.wait_ge(pool_cst, 3)
            for i in range(4):
                r = HD * (i % 2)
                pool.dma_start(POOL_W[i // 2][r:r + HD, r:r + HD], w["pool_w_2"][0, i]).then_inc(pool_in, 16)
            for h in range(8):
                src = scratch[h].rearrange("q l -> (q l)")[P - 1:P - 1 + P * (REL_L - 1)]
                pool.dma_start(G[:, h, :], src.rearrange("(q l) -> q l", l=REL_L - 1)[:, 0:S]).then_inc(rel_in, 16)
            vectors(4, w["g_mix_post_2"][0], w["g_ffn_pre_2"][0])
            pool.dma_start(misc[:, 0:D].rearrange("p (t n) -> p t n", t=T),
                           w["p_2"][0, 0].rearrange("(t p) n -> p t n", p=P)).then_inc(p_in, 16)
            vectors(5, w["g_ffn_post_2"][0], w["g_ple_2"][0])


_INS = ["x", "ln_g", "ln_b", "mla_w_in", "mla_q_norm", "mla_w_q_up", "mla_kv_norm", "mla_w_kv_up", "mla_w_out",
        "swa_w_in", "swa_sinks", "swa_w_out", "fox_w_in", "fox_b_f", "fox_w_out", "p_2", "rel_bias_2", "g_mix_pre_2",
        "w_in_2", "conv_w_2", "pool_w_2", "pool_scale_2", "w_out_2", "g_mix_post_2", "g_ffn_pre_2", "w_gate_up_2",
        "w_down_2", "g_ffn_post_2", "g_ple_2", "w_ple_gate_2", "w_ple_proj_2"]


def tables():
    f = np.float32
    q, k = np.arange(P)[:, None], np.arange(P)[None, :]
    zmask = np.zeros((P, S), f)
    zmask[:, S - P:] = np.where(k <= q, f(0), f(NEG))
    tri = np.ones((P, S), f)
    tri[:, 0:P] = (k >= q).astype(f)
    inv = f(10000.0) ** (-np.arange(0, ROPE, 2, dtype=f) / f(ROPE))
    ang = (np.arange(S, dtype=f)[:, None] * inv[None, :]).T.astype(f)
    cos, sin = np.cos(ang).astype(f), np.sin(ang).astype(f)
    rope = np.concatenate([cos, cos, -sin, sin])
    dist = q + P - np.arange(2 * P)[None, :]
    window = np.where((dist >= 0) & (dist < P), dist, BIG).astype(f)
    counts = np.zeros((P, 2, S), f)
    for i, n in enumerate((2, 4, 8, 16)):
        counts[HD * (i % 2):HD * (i % 2) + HD, i // 2, :] = f(1) / np.minimum(np.arange(S) + 1, n).astype(f)
    d = S - 1 - np.arange(REL_L)
    exact = BUCKETS // 2
    large = exact + (np.log(np.maximum(d, 1).astype(f) / f(exact)) / f(np.log(P / exact)) * f(BUCKETS - exact)).astype(np.int32)
    bucket = np.where(d < exact, np.maximum(d, 0), np.minimum(large, BUCKETS - 1))
    onehot = np.zeros((BUCKETS + 1, REL_L), f)
    onehot[bucket[d >= 0], np.nonzero(d >= 0)[0]] = 1.0
    onehot[BUCKETS, d < 0] = NEG
    return {"ident": np.eye(P, dtype=f), "zmask": zmask, "tri": tri, "rope": rope, "window": window, "counts": counts,
            "onehot": onehot}


def kernel(**inputs):
    cols = {n: np.asarray(inputs[n]) for n in ("mla_q_norm", "mla_kv_norm", "fox_b_f", "pool_scale_2", "rel_bias_2", "conv_w_2")}
    inputs = dict(inputs)
    inputs["mla_q_norm"] = cols["mla_q_norm"].reshape(2, 3, P).transpose(2, 0, 1)
    inputs["mla_kv_norm"] = cols["mla_kv_norm"].reshape(2, 2, P).transpose(2, 0, 1)
    inputs["fox_b_f"] = cols["fox_b_f"].reshape(HEADS, 1)
    inputs["pool_scale_2"] = cols["pool_scale_2"].reshape(2, P).T
    inputs["rel_bias_2"] = cols["rel_bias_2"].T
    inputs["conv_w_2"] = cols["conv_w_2"].reshape(3, 2, P).transpose(2, 1, 0)
    import concourse.bacc as _bacc
    from concourse.bass_utils import run_bass_kernel_spmd as _run

    nc = _bacc.Bacc("TRN2", target_bir_lowering=False, num_devices=1)
    arrays, w, consts = {}, {}, {}
    for group, names in ((w, {n: inputs[n] for n in _INS}), (consts, tables())):
        for name, value in names.items():
            a = np.ascontiguousarray(value)
            arrays[f"in_{name}_dram"] = a
            group[name] = nc.dram_tensor(f"in_{name}_dram", a.shape, mybir.dt.from_np(a.dtype), kind="ExternalInput").ap()
    out = nc.dram_tensor("out_dram", (1, S, D), F32, kind="ExternalOutput").ap()
    build(nc, w, consts, out)
    r = _run(nc, [arrays], core_ids=[0])
    return r.results[0]["out_dram"]
```

```python
from contextlib import ExitStack

import numpy as np

import concourse.bass as bass
from concourse import mybir

F32 = mybir.dt.float32
F32R = mybir.dt.float32r
I32 = mybir.dt.int32
ALU = mybir.AluOpType
ACT = mybir.ActivationFunctionType

P = 128
S = 512
T = S // P
D = 1024
KD = D // P
DEPTH = 4
ALPHA = (2 * DEPTH) ** 0.25
LN_EPS = 1e-5
RMS_EPS = 1e-6
NEG = -1e30
BIG = 1e32
HD = 64
HEADS = 16
GROUP = 4
ROPE = 32
QH = HD + ROPE
QR, KVR = 384, 256
MLA_SCALE = float(QH) ** -0.5
SCALE = float(HD) ** -0.5
D_FF = 2816
KF = D_FF // P
KF_A = 16
TOPK = min(256, S // 4)
IDX_HEADS = 8
IDX_SCALE = (IDX_HEADS ** -0.5) * (64 ** -0.5)
TAKEN = -3e38
REL_L = 640
BUCKETS = 32

RING = 4
RAW = 3
LEAD = 3
UNIT = 1024

CAUSAL_KEYS = [128, 256, 384, 512]
WINDOW_KEYS = [128, 256, 256, 256]
MLA_GATES = [(5, 6, 7, 0), {1: (1, 2), 2: (3, 4)}]


def reads(src, c0, c1):
    return src[:, c0:c1].rearrange("(k p) n -> p k n", p=P)


def plan_units(w):
    units = []

    def tile(name, src, c0, n=P):
        units.append((name, KD, n, [(None, 0, n, reads(src, c0, c0 + n))], 0))

    def values(src, c0):
        for half in range(2):
            units.append(("v", KD // 2, 256, [(None, 0, 256, reads(src[half * 512:(half + 1) * 512, :], c0, c0 + 256))], 0))

    def rows(name, src, n, first=0):
        for k in range(first, first + n):
            units.append((name, 1, D, [(0, 0, D, src[k * P:(k + 1) * P, :])], 0))

    def mla(j):
        w_in, wq, wkv = w["mla_w_in"][j], w["mla_w_q_up"][j], w["mla_w_kv_up"][j]
        for i in range(5):
            tile("c", w_in, i * P)
        units.append(("krope", KD, P, [(None, 0, QH, reads(w_in, QR + KVR - HD, QR + KVR + ROPE))], 1))
        def gate(i):
            tile("gate", w_in, QR + KVR + ROPE + i * P)

        def queries(h):
            units.append(("q_up", QR // P, 2 * P,
                          [(None, i * P, QH, reads(wq, (h + i) * QH, (h + i + 1) * QH)) for i in range(2)], 1))

        for i in MLA_GATES[0]:
            gate(i)
        for g in range(HEADS // GROUP):
            queries(GROUP * g)
            for i in MLA_GATES[1].get(g, ()):
                gate(i)
            loads = []
            for k in range(KVR // P):
                src = wkv[k * P:(k + 1) * P, g * 512:(g + 1) * 512].rearrange("p (h c) -> p h c", c=2 * HD)
                loads += [(k, 0, 256, src[:, :, 0:HD]), (k, 256, 256, src[:, :, HD:2 * HD])]
            units.append(("kv_up", KVR // P, 512, loads, 0))
            queries(GROUP * g + 2)
        rows("out", w["mla_w_out"][j], KD)

    mla(0)
    swa = w["swa_w_in"][0]
    for i in range(2):
        tile("k", swa, D + i * P)
    values(swa, D + 256)
    for g in range(4):
        for i in range(2):
            tile("q", swa, (2 * g + i) * P)
            tile("gate", swa, D + 512 + (2 * g + i) * P)
    rows("out", w["swa_w_out"][0], KD)
    fox = w["fox_w_in"][0]
    tile("f", fox, 3 * D, HEADS)
    for g in range(4):
        for i in range(2):
            tile("q", fox, (2 * g + i) * P)
            tile("k", fox, D + (2 * g + i) * P)
            if i == 0:
                values(fox, 2 * D + 256 * g)
        for i in range(2):
            tile("gate", fox, 3 * D + HEADS + (2 * g + i) * P)
    rows("out", w["fox_w_out"][0], KD)
    mla(1)

    w_in = w["w_in_2"][0]
    cq, iq, ik, iw, dq = 1024, 1792, 2304, 2368, 2376
    ikv = reads(w_in, ik, ik + HD)
    units.append(("ik", KD, P, [(None, 0, HD, ikv), (None, HD, HD, ikv)], 0))
    tile("iw", w_in, iw, IDX_HEADS)
    for i in range(4):
        tile("iq", w_in, iq + i * P)
    for c in range(2):
        for part in range(3):
            tile("conv", w_in, 256 * part + c * P)
    for c in range(2):
        tile("pool", w_in, 768 + c * P)
    for base in (dq, cq):
        for i in range(2):
            tile("q", w_in, base + i * P)
            tile("k", w_in, base + 256 + i * P)
            if i == 0:
                values(w_in, base + 512)
    rows("out", w["w_out_2"][0], KD)
    for lo, hi in ((0, KF_A), (KF_A, KF)):
        for m in range(lo, hi):
            tile("ff_gate", w["w_gate_up_2"][0], m * P)
            tile("ff_up", w["w_gate_up_2"][0], D_FF + m * P)
        rows("down", w["w_down_2"][0], hi - lo, lo)
    rows("ple_gate", w["w_ple_gate_2"][0], KD)
    rows("ple_proj", w["w_ple_proj_2"][0], 2)
    return units


def build(nc, w, consts, out):
    units = plan_units(w)
    ctx = ExitStack()
    with ctx:
        def sb(name, shape, dt=F32):
            return ctx.enter_context(nc.sbuf_tensor(name, shape, dt))

        def sem(name):
            return ctx.enter_context(nc.semaphore(name))

        XTh, XTl = sb("XTh", [P, KD, S], F32R), sb("XTl", [P, KD, S], F32R)
        OTh, OTl = sb("OTh", [P, KD, S], F32R), sb("OTl", [P, KD, S], F32R)
        QKh, QKl = sb("QKh", [P, 8, S], F32R), sb("QKl", [P, 8, S], F32R)
        x_tok = sb("x_tok", [P, T, D])
        V = sb("V", [P, T, 256])
        VV = [V, sb("V_odd", [P, T, 256])]
        G = sb("G", [P, 8, S])
        PB = sb("PB", [P, 4096])
        misc = sb("misc", [P, 1152])
        w_raw = sb("w_raw", [P, RAW, UNIT])
        w_hi, w_lo = sb("w_hi", [P, RING, UNIT], F32R), sb("w_lo", [P, RING, UNIT], F32R)
        ident = sb("ident", [P, P])
        zmask = sb("zmask", [P, S])
        ones = sb("ones", [P, P])
        otmp = sb("otmp", [P, S])
        mx, nb, rs, es, ri = (sb(n, [P, 2, 4]) for n in ("mx", "nb", "rs", "es", "ri"))
        sink, nsink = sb("sink", [P, HEADS]), sb("nsink", [P, HEADS])
        qg = sb("qg", [P, 2, 5])
        bf = sb("bf", [HEADS, 1])
        st = sb("st", [P, 2, 6])
        mv = sb("mv", [P, 2])
        nt = sb("nt", [P, 1])
        sqs = sb("sqs", [P, 1])
        dev, inv = sb("dev", [P, 4, 2 * T]), sb("inv", [P, 4, 2 * T])
        eps = sb("eps", [P, 2])
        iw_t = sb("iw_t", [P, T - 1, IDX_HEADS])
        top8 = sb("top8", [P, 8])
        conv_w = sb("conv_w", [P, 2, 3])
        pool_s = sb("pool_s", [P, 2])
        rel_t = sb("rel_t", [BUCKETS + 1, 8])
        scratch = nc.dram_tensor("rel_scratch", [8, P, REL_L], F32, kind="Internal").ap()
        banks = ctx.enter_context(nc.psum_tensor("banks", [P, 8, S], F32))
        bank = [banks[:, i, :] for i in range(8)]
        S_BANK = [0, 1, 0, 2]
        S_COL = [0, 0, 128, 0]
        PT_BANK = [3, 4, 5, 4]
        PT_COL = [0, 0, 0, 384]
        PROJ = 6
        SB = [PB[:, 0:1280], PB[:, 1280:2560]]
        PT = PB[:, 2560:3840]
        vec = [PB[:, 0:1024], PB[:, 1024:2048]]
        YT = PB[:, 2048:3072]
        HT = PB[:, 3072:4096]

        raw_in = [sem(f"raw_in{i}") for i in range(RAW)]
        fixed = sem("fixed")
        hi_done = sem("hi_done")
        lo_done = sem("lo_done")
        w_mid = sem("w_mid")
        grp = sem("grp")
        bank_free = [sem("bank_free0"), sem("bank_free1")]
        g_hi = sem("g_hi")
        g_tmp = sem("g_tmp")
        s_done = sem("s_done")
        s_free = sem("s_free")
        nb_done = sem("nb_done")
        exp_done = sem("exp_done")
        p_done = sem("p_done")
        t_done = sem("t_done")
        t_free = sem("t_free")
        y_done = sem("y_done")
        y_sum = sem("y_sum")
        y3 = sem("y3")
        x_new = sem("x_new")
        dev_done = sem("dev_done")
        src_done = sem("src_done")
        xt_done = sem("xt_done")
        xt_hi, xt_lo = sem("xt_hi"), sem("xt_lo")
        x_in = [sem(f"x_in{t}") for t in range(T)]
        cst, pool_cst = sem("cst"), sem("pool_cst")
        vec_in = [sem(f"vec_in{i}") for i in range(6)]
        rope_in = [sem(f"rope_in{j}") for j in range(2)]
        win_in, tri_in, pool_in, p_in, rel_in, onehot_in, rel_dma = (
            sem(n) for n in ("win_in", "tri_in", "pool_in", "p_in", "rel_in", "onehot_in", "rel_dma"))
        aug_in = [sem(f"aug_in{p}") for p in range(2)]
        diag = sem("diag")
        ident_in = sem("ident_in")
        ln_var = sem("ln_var")
        own = sem("own")
        chain = sem("chain")
        sq_done = sem("sq_done")
        c_tmp, c_hi, c_lo = sem("c_tmp"), sem("c_hi"), sem("c_lo")
        kr_done = sem("kr_done")
        fx, fx_m = sem("fx"), sem("fx_m")
        idx_s, idx_r, idx_f = sem("idx_s"), sem("idx_r"), sem("idx_f")
        pool_r, pool_d = sem("pool_r"), sem("pool_d")
        ple_sg = sem("ple_sg")
        fin = sem("fin")
        out_done = sem("out_done")

        block = ctx.enter_context(nc.Block())

        class Count:
            def __init__(self):
                self.u = 0
                self.g = 0
                self.hi = 0
                self.tmp = 0
                self.head = 0
                self.tile = 0
                self.xt = 0
                self.src = 0
                self.own = 0
                self.cp = self.sq = self.vec = self.idx = self.aug = self.sg = 0
                self.early = False
                self.dev = 0
                self.ln = 0

        gone = []
        mark = {}
        slot_at, raw_at, fix_at, n_fix = [0] * RAW, [], [], 0
        for u, unit in enumerate(units):
            slot_at[u % RAW] += 16 * len(unit[3])
            raw_at.append(slot_at[u % RAW])
            n_fix += 2 * unit[4]
            fix_at.append(n_fix)

        def view(t, u, ring):
            _, nk, ncol, _, _ = units[u]
            return t[:, u % ring, 0:nk * ncol].rearrange("p (k n) -> p k n", k=nk)

        def groups_stored(eng, n):
            for b in range(2):
                if (n + 1 - b) // 2:
                    eng.wait_ge(bank_free[b], (n + 1 - b) // 2)

        class Head:
            def __init__(self, q, k, rows, vb, v, keys, scale, bias, dst, gate=None, sink=None, sel=False, packed=0):
                self.q, self.k, self.rows, self.vb, self.v, self.keys, self.scale = q, k, rows, VV[vb], v, keys, scale
                self.bias, self.dst, self.gate, self.sink, self.sel, self.p0 = bias, dst, gate, sink, sel, packed
                self.window = keys is WINDOW_KEYS
                self.at = [sum(keys[:t]) for t in range(T)]
                self.pn = [256, 256, 256, 128] if self.window else [512, 384, 256, 128]
                self.pt = [0, self.pn[0], self.pn[0] + self.pn[1] + 128, self.pn[0] + self.pn[1]]

            def score(self, b, t):
                return SB[b][:, self.at[t]:self.at[t] + self.keys[t]]

            def tiles(self, j):
                return range(j, min(j + 2, T) if self.window else T)

        def causal(h):
            return lambda t: zmask[:, S - CAUSAL_KEYS[t]:S]

        def o_mla(i):
            return (OTh, OTl, 5 + i) if i < 3 else (XTh, XTl, i)

        def mla_heads():
            return [Head(i % 4, 4 + i % 4, QH, i // 4 % 2, i % 4 * HD, CAUSAL_KEYS, MLA_SCALE, causal(i),
                         (*o_mla(i // 2), HD * (i % 2)), gate=i // 2) for i in range(HEADS)]

        def swa_heads():
            return [Head(i % 4, 4 + i // 4, HD, 0, i // 4 * HD, WINDOW_KEYS, SCALE,
                         lambda t, i=i: misc[:, 256 + 256 * (i % 2) + (128 if t == 0 else 0):512 + 256 * (i % 2)],
                         (OTh, OTl, i // 2, HD * (i % 2)), gate=i // 2, sink=i)
                    for i in range(HEADS)]

        def fox_heads():
            return [Head(i % 4, 4 + i % 4, HD + 2, i // 4 % 2, i % 4 * HD, CAUSAL_KEYS, SCALE, causal(i),
                         (OTh, OTl, i // 2, HD * (i % 2)), gate=i // 2) for i in range(HEADS)]

        def rel_heads():
            return [Head(i % 4, 4 + i % 4, HD, i // 4, i % 4 * HD, CAUSAL_KEYS, SCALE,
                         lambda t, h=(i + 4) % 8: G[:, h, S - CAUSAL_KEYS[t]:S],
                         (OTh, OTl, (6, 4)[i // 4] + i % 4 // 2, HD * (i % 2)), sel=i >= 4) for i in range(8)]

        SEL = [None, misc[:, 0:256], misc[:, 256:640], misc[:, 640:1152]]
        WORK = SEL
        RELU = [PB[:, 896:1408], PB[:, 1408:1920]]
        CONV_A, CONV_H, CONV_Y = PB[:, 1920:2432], PB[:, 2446:2960], PB[:, 2976:3488]
        POOL_B = [PB[:, 1920:2448], PB[:, 2448:2976], PB[:, 2976:3504]]
        POOL_W = [PB[:, 3840 + P * c:3840 + P * (c + 1)] for c in range(2)]
        FZ, FA, FE, FL = (PB[0:HEADS, S * i:S * (i + 1)] for i in range(4))
        FT = PB[:, 2048:2048 + T * HEADS].rearrange("p (t h) -> p t h", t=T)
        TRI = PB[:, 3584:4096]
        REL_1H, REL_V = PB[0:BUCKETS + 1, 3072:3712], PB[0:8, 2048:2688]
        ROT = [misc[ROPE * i:ROPE * (i + 1), 0:2 * S] for i in range(2)]
        DIAG = PB[:, 2560:3584].rearrange("p (a n) -> p a n", n=P)
        SG = [PB[:, 0:512], PB[:, 512:1024]]
        Y3 = V[:, :, :].rearrange("p a b -> p (a b)")
        V2 = V[:, :, :].rearrange("p (c a) b -> p c (a b)", c=2)
        ff_dst = [(QKh, QKl, m) if m < 8 else (OTh, OTl, m - 8) for m in range(KF_A)]
        ff_dst += [(QKh, QKl, m) for m in range(KF - KF_A)]

        CONSTANTS = [(zmask[:, :], consts["zmask"]),
                     (sink[:, :], w["swa_sinks"][0].partition_broadcast(P)),
                     (bf[:, :], w["fox_b_f"]), (pool_s[:, :], w["pool_scale_2"]), (rel_t[0:BUCKETS, :], w["rel_bias_2"]),
                     (conv_w[:, :, :], w["conv_w_2"]), (qg[:, :, 0:3], w["mla_q_norm"]), (qg[:, :, 3:5], w["mla_kv_norm"])]
        N_CST = 16 * len(CONSTANTS)

        @block.tensor
        def _(pe):
            c = Count()

            def three(o, ah, al, bh, bl, first, last):
                nc.tensor.matmul(o, ah, bh, start=first, stop=False, skip_group_check=True)
                nc.tensor.matmul(o, ah, bl, start=False, stop=False, skip_group_check=True)
                return nc.tensor.matmul(o, al, bh, start=False, stop=last, skip_group_check=True)

            def unit(name):
                assert units[c.u][0] == name, (name, units[c.u][0])
                pe.wait_ge(lo_done, c.u + 1)
                h, l = view(w_hi, c.u, RING), view(w_lo, c.u, RING)
                c.u += 1
                return h, l

            def begin():
                if c.g >= 2:
                    pe.wait_ge(bank_free[c.g % 2], c.g // 2)
                return bank[PROJ + c.g % 2]

            def end(mm):
                mm.then_inc(grp, 1)
                c.g += 1

            def released():
                gone.append((grp, c.g))

            def tile(name, n0=0, src=(XTh, XTl)):
                h, l = unit(name)
                o = begin()
                nk, m = h.shape[1], h.shape[2]
                for k in range(nk):
                    mm = three(o[0:m, 0:S - n0], h[:, k, :], l[:, k, :], src[0][:, k, n0:S], src[1][:, k, n0:S],
                               k == 0, k == nk - 1)
                end(mm)
                released()

            ready, ready_v = {}, {}

            def head_tile(name, *heads):
                tile(name)
                for h in heads:
                    ready[c.head + h] = c.g

            def values(head=0):
                parts = [unit("v"), unit("v")]
                for half in range(2):
                    o = begin()
                    for t in (2 * half, 2 * half + 1):
                        ts = slice(t * P, (t + 1) * P)
                        for k in range(KD):
                            h, l = parts[k // 4]
                            mm = three(o[:, 256 * (t % 2):256 * (t % 2) + 256], XTh[:, k, ts], XTl[:, k, ts],
                                       h[:, k % 4, :], l[:, k % 4, :], k == 0, k == KD - 1)
                    end(mm)
                released()
                released()
                ready_v[c.head + head] = c.g

            def attention(heads, between=None):
                a0 = c.head

                def scores(i):
                    hd, a = heads[i], a0 + i
                    r = slice(0, hd.rows)
                    if a in ready:
                        groups_stored(pe, ready[a])
                    if hd.rows == HD + 2 and i % 2 == 0 and i != 2:
                        pe.wait_ge(aug_in[i % 4 // 2], 16 * (4 * (i // GROUP) + (0 if i % 4 else 8)))
                    for t in (0, 2, 1, 3):
                        if t != 2 and a:
                            pe.wait_ge(s_free, 3 * (a - 1) + S_BANK[t] + 1)
                        ts = slice(t * P, (t + 1) * P)
                        ks = slice((t + 1) * P - hd.keys[t], (t + 1) * P)
                        mm = three(bank[S_BANK[t]][:, S_COL[t]:S_COL[t] + hd.keys[t]],
                                   QKh[r, hd.q, ts], QKl[r, hd.q, ts], QKh[r, hd.k, ks], QKl[r, hd.k, ks], True, True)
                        if t:
                            mm.then_inc(s_done, 1)

                def turn(i):
                    hd, a = heads[i], a0 + i
                    pe.wait_ge(p_done, a + 1)
                    for j in (0, 1, 3, 2):
                        if j != 3 and a:
                            pe.wait_ge(t_free, 3 * (a - 1) + j + 1)
                        for t in hd.tiles(j):
                            col = hd.at[t] + j * P - ((t + 1) * P - hd.keys[t])
                            o = (hd.pn[1] if j == 3 else 0) + (t - j) * P
                            mm = nc.tensor.transpose(bank[PT_BANK[j]][:, o:o + P], SB[a % 2][:, col:col + P], ident[:, :])
                        if j != 1:
                            mm.then_inc(t_done, 1)

                def mix(i):
                    hd, a = heads[i], a0 + i
                    o = begin()
                    if a in ready_v:
                        groups_stored(pe, ready_v[a])
                    pe.wait_ge(t_free, 3 * a + 3)
                    for j in range(T):
                        mm = nc.tensor.matmul(o[0:HD, j * P:j * P + hd.pn[j]], hd.vb[:, j, hd.v:hd.v + HD],
                                              PT[:, hd.pt[j]:hd.pt[j] + hd.pn[j]], start=(j == 0), stop=(j == T - 1),
                                              skip_group_check=True)
                    end(mm)

                scores(0)
                for i in range(len(heads)):
                    if i + 1 < len(heads):
                        scores(i + 1)
                    if between:
                        between(i)
                    turn(i)
                    if i:
                        mix(i - 1)
                mix(len(heads) - 1)
                c.head += len(heads)

            def row_step(k, t, src, part, first, last):
                for half in range(2):
                    ah, al = src(k, slice(t * P, (t + 1) * P))
                    hs = slice(half * S, (half + 1) * S)
                    mm = three(bank[2 * t + half][:, :], ah, al, part[0][:, 0, hs], part[1][:, 0, hs], first, last)
                return mm

            def mid(mm):
                mm.then_inc(w_mid, 1)
                c.sq += 1
                return (w_mid, c.sq)

            def out_rows(name, n, src, first=True, last=True, turned=None, lag=1):
                groups_stored(pe, c.g)
                held = RING if last else 0
                for k in range(n - held):
                    part = unit(name)
                    for t in range(T):
                        mm = row_step(k, t, src, part, k == 0 and (first or t == T - 1), False)
                    gone.append(mid(mm))
                if not last:
                    return
                parts = []
                for t in range(T):
                    for i in range(held):
                        if t == 0:
                            parts.append(unit(name))
                        mm = row_step(n - held + i, t, src, parts[i], False, i == held - 1)
                        if t == T - 1 and i < held - 1:
                            gone.append(mid(mm))
                    mm.then_inc(y_done, 1)
                    c.tile += 1
                    if t >= lag:
                        turn_tile(t - lag, turned)
                gone.append((y_done, c.tile))
                for t in range(T - lag, T):
                    turn_tile(t, turned)
                pe.wait_ge(xt_lo, c.xt)

            def turn_tile(t, src, ready=None):
                if ready is None:
                    pe.wait_ge(src_done, c.src + 1)
                    c.src += 1
                else:
                    pe.wait_ge(*ready)
                for half in range(2):
                    for i in range(4):
                        ch = 4 * half + i
                        mm = nc.tensor.transpose(bank[2 * t + half][:, i * P:(i + 1) * P],
                                                 src(t)[:, ch * P:(ch + 1) * P], ident[:, :])
                    mm.then_inc(xt_done, 1)
                    c.xt += 1

            def of(*tiles):
                return lambda k, ts: (tiles[0][:, k, ts], tiles[1][:, k, ts])

            def mla(j):
                for i in range(5):
                    tile("c")
                tile("krope")
                o = begin()
                pe.wait_ge(sq_done, 5 * (j + 1))
                for t in range(T):
                    for n, (lo, hi) in enumerate(((0, 3), (3, 5))):
                        for k in range(lo, hi):
                            mm = nc.tensor.matmul(o[:, T * n + t:T * n + t + 1],
                                                  PB[:, S * k + t * P:S * k + (t + 1) * P], ones[:, 0:1],
                                                  start=(k == lo), stop=(k == hi - 1), skip_group_check=True)
                end(mm)
                tile("gate")
                tile("gate")
                pe.wait_ge(diag, j + 1)
                for n in range(2):
                    o = begin()
                    for t in range(T):
                        mm = nc.tensor.matmul(o[:, t * P:(t + 1) * P], ones[:, :], DIAG[:, T * n + t, :], start=True,
                                              stop=True, skip_group_check=True)
                    end(mm)
                tile("gate")
                tile("gate")
                pe.wait_ge(c_lo, 5 * (j + 1))

                def queries(h0):
                    h, l = unit("q_up")
                    for i in range(2):
                        o = begin()
                        for k in range(3):
                            mm = three(o[:, :], h[:, k, i * P:(i + 1) * P], l[:, k, i * P:(i + 1) * P],
                                       OTh[:, k, :], OTl[:, k, :], k == 0, k == 2)
                        end(mm)
                    released()
                    ready[c.head + h0] = c.g

                def keys_values(h0):
                    h, l = unit("kv_up")
                    for pair in range(2):
                        o = begin()
                        for k in range(2):
                            mm = three(o[:, :], h[:, k, pair * P:(pair + 1) * P], l[:, k, pair * P:(pair + 1) * P],
                                       OTh[:, 3 + k, :], OTl[:, 3 + k, :], k == 0, k == 1)
                        end(mm)
                    for half in range(2):
                        o = begin()
                        for t in (2 * half, 2 * half + 1):
                            ts = slice(t * P, (t + 1) * P)
                            for k in range(2):
                                mm = three(o[:, 256 * (t % 2):256 * (t % 2) + 256], OTh[:, 3 + k, ts], OTl[:, 3 + k, ts],
                                           h[:, k, 256:512], l[:, k, 256:512], k == 0, k == 1)
                        end(mm)
                    released()
                    ready[c.head + h0] = ready_v[c.head + h0] = c.g

                def between(i):
                    g, step = i // GROUP + 1, i % GROUP
                    if g == GROUP:
                        return
                    if step == 0:
                        queries(GROUP * g)
                    if step < len(MLA_GATES[1].get(g, ())):
                        tile("gate")
                    if step == 2:
                        keys_values(GROUP * g)
                    if step == 3:
                        queries(GROUP * g + 2)

                queries(0)
                keys_values(0)
                queries(2)
                pe.wait_ge(kr_done, 6 * (j + 1))
                attention(mla_heads(), between)
                out_rows("out", KD, lambda k, ts: tuple(part[:, o_mla(k)[2], ts] for part in o_mla(k)[:2]), turned=(lambda t: HT) if j else (lambda t: x_tok[:, t, :]),
                         lag=2 if j else 1)

            pe.wait_ge(ident_in, 16)
            for t in range(T):
                turn_tile(t, lambda t: x_tok[:, t, :], (x_in[t], 16))
            pe.wait_ge(xt_lo, c.xt)
            pe.wait_ge(onehot_in, 16)
            pe.wait_ge(cst, N_CST)
            pe.wait_ge(pool_cst, 2)
            for n in range(2):
                o = begin()
                nn = 512 if n == 0 else REL_L - 512
                end(nc.tensor.matmul(o[0:8, 0:nn], rel_t[:, :], REL_1H[:, n * 512:n * 512 + nn], start=True, stop=True))
            mla(0)
            for i in range(2):
                tile("k")
            values()

            def between(i):
                if i < HEADS - GROUP:
                    if i % 2 == 0:
                        head_tile("q", i + GROUP, i + GROUP + 1)
                    else:
                        tile("gate")

            for i in range(GROUP):
                between(i - GROUP)
            attention(swa_heads(), between)
            out_rows("out", KD, of(OTh, OTl), turned=lambda t: x_tok[:, t, :])
            tile("f")
            o = begin()
            pe.wait_ge(fx, 1)
            for t in range(T):
                mm = nc.tensor.transpose(o[:, HEADS * t:HEADS * (t + 1)], FL[:, t * P:(t + 1) * P], ident[0:HEADS, 0:HEADS])
            end(mm)
            o = begin()
            groups_stored(pe, c.g)
            pe.wait_ge(tri_in, 16)
            for t in range(T):
                mm = nc.tensor.matmul(o[0:HEADS, t * P:S], FT[:, t, :], TRI[:, 0:S - t * P], start=(t == 0), stop=(t == T - 1),
                                      skip_group_check=True)
            end(mm)

            def between(i):
                if i < HEADS - GROUP:
                    h, step = i + GROUP, i % GROUP
                    if step % 2 == 0:
                        head_tile("q", h, h + 1)
                        head_tile("k", h, h + 1)
                    elif step == 1:
                        values(h - 1)
                    else:
                        tile("gate")
                        tile("gate")

            for i in range(GROUP):
                between(i - GROUP)
            attention(fox_heads(), between)
            out_rows("out", KD, of(OTh, OTl), turned=lambda t: x_tok[:, t, :])
            mla(1)
            tile("ik")
            h, l = unit("iw")
            o = begin()
            for t in range(1, T):
                for k in range(KD):
                    ts = slice(t * P, (t + 1) * P)
                    mm = three(o[:, IDX_HEADS * (t - 1):IDX_HEADS * t], XTh[:, k, ts], XTl[:, k, ts],
                               h[:, k, :], l[:, k, :], k == 0, k == KD - 1)
            end(mm)
            released()
            for i in range(4):
                tile("iq", n0=P)
            groups_stored(pe, c.g)
            for t in range(1, T):
                for h in range(IDX_HEADS):
                    n = c.idx
                    if n >= 2:
                        pe.wait_ge(idx_r, n - 1)
                    r = slice(HD * (h % 2), HD * (h % 2) + HD)
                    qs = slice((t - 1) * P, t * P)
                    keys = CAUSAL_KEYS[t]
                    three(bank[n % 2][:, 0:keys], QKh[r, h // 2, qs], QKl[r, h // 2, qs],
                          QKh[r, 4, 0:keys], QKl[r, 4, 0:keys], True, True).then_inc(idx_s, 1)
                    c.idx += 1
            for cc in range(2):
                for part in range(3):
                    tile("conv")
            for cc in range(2):
                tile("pool")
                o = begin()
                pe.wait_ge(pool_d, cc + 1)
                if cc == 0:
                    pe.wait_ge(pool_in, 80)
                end(nc.tensor.matmul(o[:, :], POOL_W[cc], POOL_B[0][:, 16:528], start=True, stop=True))

            def between(i):
                if i < GROUP:
                    h, step = i + GROUP, i % GROUP
                    if step % 2 == 0:
                        head_tile("q", h, h + 1)
                        head_tile("k", h, h + 1)
                    elif step == 1:
                        values(h - 1)

            for i in range(GROUP):
                between(i - GROUP)
            attention(rel_heads(), between)
            out_rows("out", KD, of(OTh, OTl), turned=lambda t: HT, lag=2)
            for lo, hi in ((0, KF_A), (KF_A, KF)):
                for m in range(lo, hi):
                    tile("ff_gate")
                    tile("ff_up")
                out_rows("down", hi - lo, lambda k, ts: (ff_dst[lo + k][0][:, ff_dst[lo + k][2], ts],
                                                         ff_dst[lo + k][1][:, ff_dst[lo + k][2], ts]),
                         first=lo == 0, last=lo > 0, turned=lambda t: HT, lag=2)
                if lo == 0:
                    mark["y3"] = c.sq
                    pe.wait_ge(y3, 2)
            for cc in range(2):
                o = begin()
                pe.wait_ge(p_in, 16)
                for t in range(T):
                    mm = nc.tensor.transpose(o[:, t * P:(t + 1) * P], misc[:, 256 * t + cc * P:256 * t + (cc + 1) * P], ident[:, :])
                end(mm)
            groups_stored(pe, c.g)
            src = of(XTh, XTl)
            for k in range(KD - 2):
                part = unit("ple_gate")
                for t in range(T):
                    mm = row_step(k, t, src, part, k == 0, False)
                gone.append(mid(mm))
            parts = []

            def project(t):
                pe.wait_ge(ple_sg, t + 1)
                for i in range(2):
                    mm = row_step(i, t, of(QKh, QKl), parts[2 + i], i == 0, i == 1)
                mm.then_inc(y_done, 1)
                c.tile += 1

            for t in range(T):
                for i in range(2):
                    if t == 0:
                        parts.append(unit("ple_gate"))
                    mm = row_step(KD - 2 + i, t, src, parts[i], False, i == 1)
                if t == 0:
                    parts += [unit("ple_proj"), unit("ple_proj")]
                mm.then_inc(y_done, 1)
                c.tile += 1
                if t:
                    project(t - 1)
            project(T - 1)
            gone.extend([(y_done, c.tile)] * 4)

        NU = len(gone)

        @block.sync
        def _(sp):
            sp.dma_start(ident[:, :], consts["ident"]).then_inc(ident_in, 16)
            for t in range(T):
                sp.dma_start(x_tok[:, t, :], w["x"][0, t * P:(t + 1) * P, :]).then_inc(x_in[t], 16)
            for u in range(NU):
                if u >= RAW:
                    sp.wait_ge(lo_done, u - RAW + 1)
                for k, c0, n, src in units[u][3]:
                    dst = view(w_raw, u, RAW)
                    if k is None:
                        dst = dst[:, :, c0:c0 + n]
                    else:
                        dst = dst[:, k, c0:c0 + n]
                        if len(src.shape) == 3:
                            dst = dst.rearrange("p (h c) -> p h c", c=HD)
                    sp.dma_start(dst, src).then_inc(raw_in[u % RAW], 16)
            for t in range(T):
                sp.wait_ge(fin, t + 1)
                sp.dma_start(out[0, t * P:(t + 1) * P, :], x_tok[:, t, :]).then_inc(out_done, 16)
            sp.wait_ge(out_done, 16 * T)

        @block.scalar
        def _(act):
            c = Count()

            def split(u):
                if u >= NU:
                    return
                act.wait_ge(raw_in[u % RAW], raw_at[u])
                if units[u][4]:
                    act.wait_ge(fixed, fix_at[u])
                if u >= RING:
                    act.wait_ge(*gone[u - RING])
                nc.scalar.activation(view(w_hi, u, RING), view(w_raw, u, RAW), ACT.Copy).then_inc(hi_done, 1)

            def early():
                split(c.u + LEAD)
                c.early = True

            def advance(n=1):
                for _ in range(n):
                    if not c.early:
                        split(c.u + LEAD)
                    c.early = False
                    c.u += 1

            def vectors(i, *names):
                groups_stored(act, c.g)
                for n, v in enumerate(names):
                    dst = vec[n] if n < 2 else V[:, :, :].rearrange("p a b -> p (a b)")
                    act.dma_start(dst, v.partition_broadcast(P)).then_inc(vec_in[i], 16)

            def group():
                act.wait_ge(grp, c.g + 1)
                c.g += 1
                return bank[PROJ + (c.g - 1) % 2]

            def stored(ins):
                ins.then_inc(bank_free[(c.g - 1) % 2], 1)

            def hi(dst, src, scale=1.0):
                nc.scalar.activation(dst, src, ACT.Copy, scale=scale).then_inc(g_hi, 1)
                c.hi += 1

            def pair(slot):
                o = group()
                hi(QKh[0:HD, slot, :], o[0:HD, :])
                hi(QKh[0:HD, slot + 1, :], o[HD:P, :])

            def slots_free(i):
                if i >= 0:
                    act.wait_ge(s_done, 3 * (c.head + i + 1))

            def rotary(o, slot, nope=True):
                act.wait_ge(g_tmp, c.tmp + 1)
                c.tmp += 1
                r = slice(0 if nope else HD, QH)
                hi(QKh[r, slot, :], o[r, :])

            def values(half, vb=0):
                o = group()
                stored(nc.scalar.activation(VV[vb][:, 2 * half:2 * half + 2, :], o[:, :].rearrange("p (t n) -> p t n", t=2), ACT.Copy))

            def value_units(vb=0):
                advance()
                for half in range(2):
                    values(half, vb)
                advance()

            def gate(i):
                o = group()
                nc.scalar.activation(G[:, i, :], o[:, :], ACT.Tanh, scale=0.5).then_inc(g_hi, 1)
                c.hi += 1

            def from_tmp(dst, src=None):
                act.wait_ge(g_tmp, c.tmp + 1)
                c.tmp += 1
                hi(dst, otmp[:, :] if src is None else src)

            def attention(heads, between=None):
                a0 = c.head

                def exps(i):
                    hd, a = heads[i], a0 + i
                    b = a % 2
                    act.wait_ge(nb_done, a + 1)
                    for t in range(T):
                        sc = hd.score(b, t)
                        ins = nc.scalar.activation(sc, sc, ACT.Exp, bias=nb[:, b, t:t + 1], scale=hd.scale,
                                                   accum_out=rs[:, b, t:t + 1])
                    if hd.sink is not None:
                        ins = nc.scalar.activation(es[:, b, :], nb[:, b, :], ACT.Exp, bias=sink[:, hd.sink:hd.sink + 1])
                    ins.then_inc(exp_done, 1)

                def turned(i):
                    hd, a = heads[i], a0 + i
                    if i:
                        act.wait_ge(grp, c.g + 1)
                    for n, j in enumerate((0, 1, 2)):
                        act.wait_ge(t_done, 3 * a + n + 1)
                        width = hd.pn[j] + (P if j == 1 else 0)
                        nc.scalar.activation(PT[:, hd.pt[j]:hd.pt[j] + width], bank[PT_BANK[j]][:, 0:width], ACT.Copy)\
                            .then_inc(t_free, 1)

                def store(i):
                    hd = heads[i]
                    h, l, ch, r0 = hd.dst
                    o = group()
                    if hd.gate is None:
                        hi(h[r0:r0 + HD, ch, :], o[0:HD, :])
                    else:
                        from_tmp(h[r0:r0 + HD, ch, :], otmp[r0:r0 + HD, :])

                exps(0)
                for i in range(len(heads)):
                    if between:
                        between(i)
                    if i + 1 < len(heads):
                        if not c.early:
                            early()
                        exps(i + 1)
                    turned(i)
                    if i:
                        store(i - 1)
                store(len(heads) - 1)
                c.head += len(heads)

            def turned_tile(t):
                ts = slice(t * P, (t + 1) * P)
                for half in range(2):
                    act.wait_ge(xt_done, c.xt + 1)
                    c.xt += 1
                    nc.scalar.activation(XTh[:, 4 * half:4 * half + 4, ts],
                                         bank[2 * t + half][:, :].rearrange("p (k n) -> p k n", k=4), ACT.Copy)\
                        .then_inc(xt_hi, 1)

            def layer_tail():
                advance(KD - LEAD)
                c.tile += T
                for t in range(T):
                    if t:
                        turned_tile(t - 1)
                    ln_deviation()
                advance(LEAD)
                turned_tile(T - 1)

            def deviation(parts, ready=None):
                if ready:
                    act.wait_ge(*ready)
                for lo, n, src, scale, e in parts:
                    ins = nc.scalar.activation(dev[:, c.dev % 4, lo:lo + n], src, ACT.Sqrt, bias=eps[:, e:e + 1], scale=scale)
                ins.then_inc(dev_done, 1)
                c.dev += 1

            def rms(src):
                act.wait_ge(dev_done, c.dev)
                nc.scalar.activation(G[:, 0:2, :].rearrange("p a b -> p (a b)"), src, ACT.Square, accum_out=sqs[:, 0:1])\
                    .then_inc(own, 1)
                c.own += 1
                deviation([(0, 1, sqs[:, 0:1], 1.0 / D, 0)], (own, c.own))

            def x_squares(t):
                act.wait_ge(x_new, c.sq + 1)
                c.sq += 1
                rms(x_tok[:, t, :])

            def y_squares(t, last_saved):
                if last_saved and t == T - 1:
                    act.wait_ge(y_sum, 1)
                    src = YT
                else:
                    act.wait_ge(y_done, c.tile + 1)
                    src = banks[:, 2 * t:2 * t + 2, :].rearrange("p a b -> p (a b)")
                c.tile += 1
                rms(src)

            def ln_deviation():
                c.ln += 1
                deviation([(0, 1, mv[:, 1:2], 1.0, 1)], (ln_var, c.ln))

            def normed_tail(n, y=True, last_saved=False):
                advance(n - LEAD)
                for t in range(T + 2):
                    if t < T:
                        if y:
                            y_squares(t, last_saved)
                        else:
                            ln_deviation()
                    if 0 < t <= T:
                        x_squares(t - 1)
                    if t == T + 1:
                        advance(LEAD)
                    if t >= 2:
                        turned_tile(t - 2)
                if not y:
                    c.tile += T

            def mla(j):
                for i in range(5):
                    advance()
                    o = group()
                    if i == 4 and j == 0:
                        act.wait_ge(rel_dma, 16)
                    nc.scalar.activation(PB[:, S * i:S * (i + 1)], o[:, :], ACT.Square).then_inc(sq_done, 1)
                    stored(nc.scalar.activation(G[:, i, :], o[:, :], ACT.Copy))
                advance()
                rotary(group(), 4, nope=False)
                for s in range(3):
                    if s == 0:
                        act.wait_ge(g_hi, c.hi)
                    nc.scalar.activation(QKh[HD:QH, 5 + s, :], QKh[HD:QH, 4, :].bitcast(F32), ACT.Copy).then_inc(kr_done, 1)
                o = group()
                deviation([(0, T, o[:, 0:T], 1.0 / QR, 0), (T, T, o[:, T:2 * T], 1.0 / KVR, 0)])
                for i in MLA_GATES[0][:2]:
                    advance()
                    gate(i)
                c.g += 2
                for i in range(5):
                    act.wait_ge(c_tmp, 5 * j + i + 1)
                    nc.scalar.activation(OTh[:, i, :], G[:, i, :], ACT.Copy).then_inc(c_hi, 1)
                advance()
                gate(MLA_GATES[0][2])
                act.wait_ge(c_lo, 5 * (j + 1))
                advance()
                gate(MLA_GATES[0][3])

                def queries(h):
                    slots_free(h - 3)
                    advance()
                    for i in range(2):
                        rotary(group(), (h + i) % GROUP)

                def keys_values(h):
                    slots_free(h - 1)
                    advance()
                    for p2 in range(2):
                        pair(4 + 2 * p2)
                    for half in range(2):
                        values(half, h // GROUP % 2)

                def between(i):
                    g, step = i // GROUP + 1, i % GROUP
                    if g == GROUP:
                        return
                    if step == 0:
                        queries(GROUP * g)
                    gates = MLA_GATES[1].get(g, ())
                    if step < len(gates):
                        advance()
                        gate(gates[step])
                    if step == 2:
                        keys_values(GROUP * g)
                    if step == 3:
                        queries(GROUP * g + 2)

                queries(0)
                keys_values(0)
                queries(2)
                attention(mla_heads(), between)
                vectors(3 * j, w["ln_g"][3 * j], w["ln_b"][3 * j], *([w["g_mix_pre_2"][0]] if j else []))
                if j:
                    normed_tail(KD, y=False)
                else:
                    layer_tail()

            for t in range(T):
                turned_tile(t)
            for u in range(LEAD):
                split(u)
            act.wait_ge(pool_cst, 2)
            for n in range(2):
                o = group()
                nn = 512 if n == 0 else REL_L - 512
                stored(nc.scalar.activation(REL_V[:, n * 512:n * 512 + nn], o[0:8, 0:nn], ACT.Copy, scale=1.0 / SCALE))
            groups_stored(act, c.g)
            act.dma_start(scratch, REL_V[:, None, 0:REL_L].to_broadcast([8, P, REL_L])).then_inc(rel_dma, 16)
            mla(0)
            act.wait_ge(xt_lo, c.xt)
            act.dma_start(misc[:, 0:256], consts["window"]).then_inc(win_in, 16)
            for i in range(2):
                advance()
                pair(4 + 2 * i)
            value_units()

            def between(i):
                if i < HEADS - GROUP:
                    advance()
                    if i % 2 == 0:
                        slots_free(i + 1)
                        pair((i + GROUP) % GROUP)
                    else:
                        gate((i + GROUP) // 2)

            for i in range(GROUP):
                between(i - GROUP)
            attention(swa_heads(), between)
            vectors(1, w["ln_g"][1], w["ln_b"][1])
            layer_tail()
            act.wait_ge(xt_lo, c.xt)
            act.dma_start(misc[HD:P, 0:S], consts["rope"]).then_inc(rope_in[1], 16)
            act.dma_start(TRI, consts["tri"]).then_inc(tri_in, 16)
            advance()
            o = group()
            act.wait_ge(cst, N_CST)
            stored(nc.scalar.activation(FZ, o[0:HEADS, :], ACT.Identity, bias=bf[:, 0:1]))
            groups_stored(act, c.g)
            nc.scalar.activation(FA, FZ, ACT.Abs).then_inc(own, 1)
            act.wait_ge(own, c.own + 1)
            nc.scalar.activation(FE, FA, ACT.Exp, scale=-1.0).then_inc(own, 1)
            act.wait_ge(own, c.own + 2)
            nc.scalar.activation(FA, FE, ACT.Ln, bias=1.0).then_inc(own, 1)
            c.own += 3
            o = group()
            stored(nc.scalar.activation(FT, o[:, 0:T * HEADS].rearrange("p (t h) -> p t h", t=T), ACT.Copy))
            o = group()
            hi(OTh[0:HEADS, 7, :], o[0:HEADS, :], scale=1.0 / SCALE)
            hi(OTh[0:HEADS, 6, :], o[0:HEADS, :], scale=-1.0 / SCALE)

            def gate_rows(g, p):
                h, n = GROUP * g + 2 * p, 2 if g else GROUP
                for dst, src in ((QKh[64:65, 2 * p:2 * p + n, :], OTh[h:h + n, 7, :]),
                                 (QKl[64:65, 2 * p:2 * p + n, :], OTl[h:h + n, 7, :]),
                                 (QKh[65:66, 4 + 2 * p:4 + 2 * p + n, :], OTh[h:h + n, 6, :]),
                                 (QKl[65:66, 4 + 2 * p:4 + 2 * p + n, :], OTl[h:h + n, 6, :])):
                    act.dma_start(dst.bitcast(F32), src.bitcast(F32)).then_inc(aug_in[p], 16)

            groups_stored(act, c.g)
            act.wait_ge(fx_m, 2)
            act.wait_ge(g_hi, c.hi)
            gate_rows(0, 0)
            for dst, src in ((QKh, OTh[32:36, 7, :]), (QKl, OTl[32:36, 7, :])):
                act.dma_start(dst[65:66, 0:4, :].bitcast(F32), src.bitcast(F32)).then_inc(aug_in[0], 16)
                act.dma_start(dst[64:65, 4:8, :].bitcast(F32), src.bitcast(F32)).then_inc(aug_in[0], 16)

            def between(i):
                if i < HEADS - GROUP:
                    h, step = i + GROUP, i % GROUP
                    if step % 2 == 0:
                        slots_free(i + 1)
                        if i >= 0:
                            gate_rows(h // GROUP, step // 2)
                        for slot in (step, 4 + step):
                            advance()
                            pair(slot)
                    elif step == 1:
                        value_units(h // GROUP % 2)
                    else:
                        for n in (h // 2 - 1, h // 2):
                            advance()
                            gate(n)

            for i in range(GROUP):
                between(i - GROUP)
            attention(fox_heads(), between)
            vectors(2, w["ln_g"][2], w["ln_b"][2])
            layer_tail()
            mla(1)
            act.wait_ge(xt_lo, c.xt)
            act.dma_start(V2, consts["counts"]).then_inc(pool_in, 16)
            nc.scalar.activation(PB[:, 3840:4096], zmask[:, 0:256], ACT.Copy).then_inc(own, 1)
            c.own += 1
            act.wait_ge(own, c.own)
            for i in range(4):
                r = HD * (i % 2)
                act.dma_start(POOL_W[i // 2][r:r + HD, r:r + HD], w["pool_w_2"][0, i]).then_inc(pool_in, 16)
            for h in range(8):
                src = scratch[h].rearrange("q l -> (q l)")[P - 1:P - 1 + P * (REL_L - 1)]
                act.dma_start(G[:, h, :], src.rearrange("(q l) -> q l", l=REL_L - 1)[:, 0:S]).then_inc(rel_in, 16)
            advance()
            hi(QKh[:, 4, :], group()[:, :])
            advance()
            stored(nc.scalar.activation(iw_t[:, :, :], group()[:, 0:3 * IDX_HEADS].rearrange("p (t h) -> p t h", t=3), ACT.Copy))
            for i in range(4):
                advance()
                hi(QKh[:, i, 0:S - P], group()[:, 0:S - P])
            for t in range(1, T):
                for h in range(IDX_HEADS):
                    n = c.idx
                    act.wait_ge(idx_s, n + 1)
                    if n >= 2:
                        act.wait_ge(idx_f, n - 1)
                    keys = CAUSAL_KEYS[t]
                    nc.scalar.activation(RELU[n % 2][:, 0:keys], bank[n % 2][:, 0:keys], ACT.Relu).then_inc(idx_r, 1)
                    c.idx += 1
            for cc in range(2):
                advance()
                stored(nc.scalar.activation(CONV_A, group()[:, :], ACT.Copy))
                advance()
                c.g += 1
                advance()
                c.g += 1
                from_tmp(OTh[:, cc, :])
            for cc in range(2):
                advance()
                o = group()
                act.wait_ge(pool_r, 1 + cc)
                stored(nc.scalar.activation(POOL_B[0][:, 16:528], o[:, :], ACT.Copy))
                c.g += 1
                from_tmp(OTh[:, 2 + cc, :])

            def between(i):
                if i < GROUP:
                    h, step = i + GROUP, i % GROUP
                    if step % 2 == 0:
                        slots_free(i + 1)
                        for slot in (step, 4 + step):
                            advance()
                            pair(slot)
                    elif step == 1:
                        value_units(h // GROUP % 2)

            for i in range(GROUP):
                between(i - GROUP)
            attention(rel_heads(), between)
            vectors(4, w["g_mix_post_2"][0], w["g_ffn_pre_2"][0])
            act.dma_start(misc[:, 0:D].rearrange("p (t n) -> p t n", t=T),
                          w["p_2"][0, 0].rearrange("(t p) n -> p t n", p=P)).then_inc(p_in, 16)
            normed_tail(KD)
            for lo, hi_m in ((0, KF_A), (KF_A, KF)):
                for m in range(lo, hi_m):
                    advance()
                    stored(nc.scalar.activation(SG[m % 2], group()[:, :], ACT.Silu))
                    advance()
                    c.g += 1
                    h, l, ch = ff_dst[m]
                    from_tmp(h[:, ch, :])
                if lo == 0:
                    advance(hi_m)
                    act.wait_ge(w_mid, mark["y3"])
                    for half in range(2):
                        nc.scalar.activation(Y3[:, half * S:half * S + S], bank[6 + half][:, :], ACT.Copy).then_inc(y3, 1)
            vectors(5, w["g_ffn_post_2"][0], w["g_ple_2"][0])
            normed_tail(KF - KF_A, last_saved=True)
            for cc in range(2):
                hi(QKh[:, cc, :], group()[:, :])
            advance(KD + 2)
            for t in range(T):
                act.wait_ge(y_done, c.tile + max(1, 2 * t))
                for half in range(2):
                    ins = nc.scalar.activation(G[:, 2 * t + half, :], bank[2 * t + half][:, :], ACT.Sigmoid)
                ins.then_inc(ple_sg, 1)

        @block.vector
        def _(dve):
            c = Count()

            def link(ins):
                ins.then_inc(chain, 1)
                c.own += 1
                dve.wait_ge(chain, c.own)

            def group():
                dve.wait_ge(grp, c.g + 1)
                c.g += 1
                return bank[PROJ + (c.g - 1) % 2]

            def stored(ins):
                ins.then_inc(bank_free[(c.g - 1) % 2], 1)

            def lo(dst, src, h):
                c.hi += 1
                dve.wait_ge(g_hi, c.hi)
                return nc.vector.tensor_tensor(dst, src, h.bitcast(F32), ALU.subtract)

            def pair(slot):
                o = group()
                lo(QKl[0:HD, slot, :], o[0:HD, :], QKh[0:HD, slot, :])
                stored(lo(QKl[0:HD, slot + 1, :], o[HD:P, :], QKh[0:HD, slot + 1, :]))

            def slots_free(i):
                if i >= 0:
                    dve.wait_ge(s_done, 3 * (c.head + i + 1))

            def rotate(i):
                o = group()
                ra, rb = ROT[i][:, 0:S], ROT[i][:, S:2 * S]
                nc.vector.tensor_tensor(ra, o[HD:QH, :], misc[HD:QH, 0:S], ALU.mult)
                link(nc.vector.tensor_tensor(rb, o[QH:P, :], misc[QH:P, 0:S], ALU.mult))
                nc.vector.tensor_tensor(o[HD:QH, :], ra, rb, ALU.add).then_inc(g_tmp, 1)
                return o, c.g

            def rotated(o, g, slot, nope=True):
                r = slice(0 if nope else HD, QH)
                lo(QKl[r, slot, :], o[r, :], QKh[r, slot, :]).then_inc(bank_free[(g - 1) % 2], 1)

            def gate(i):
                o = group()
                c.hi += 1
                dve.wait_ge(g_hi, c.hi)
                stored(nc.vector.scalar_tensor_tensor(G[:, i, :], G[:, i, :], 1.0, o[:, :], ALU.add, ALU.mult))

            def inverse(n=1):
                dve.wait_ge(dev_done, c.dev + 1)
                r = inv[:, c.dev % 4, 0:n]
                link(nc.vector.reciprocal(r, dev[:, c.dev % 4, 0:n]))
                c.dev += 1
                return r

            def attention(heads, between=None):
                a0 = c.head

                def maxima(i):
                    hd, a = heads[i], a0 + i
                    b = a % 2
                    if a >= 2:
                        dve.wait_ge(t_done, 3 * (a - 1))
                    if hd.window:
                        slope = 2.0 ** (-8.0 * (hd.sink + 1) / HEADS)
                        link(nc.vector.tensor_scalar(misc[:, 256 + 256 * (i % 2):512 + 256 * (i % 2)], misc[:, 0:256],
                                                     -slope / hd.scale, None, ALU.mult))
                    for t in (0, 2, 1, 3):
                        dve.wait_ge(s_done, 3 * a + S_BANK[t] + 1)
                        o = bank[S_BANK[t]][:, S_COL[t]:S_COL[t] + hd.keys[t]]
                        if hd.sel and t:
                            link(nc.vector.tensor_tensor(hd.score(b, t), o, hd.bias(t), ALU.add))
                            ins = nc.vector.tensor_tensor_reduce(hd.score(b, t), hd.score(b, t), SEL[t], 1.0, -3e38,
                                                                 ALU.add, ALU.max, mx[:, b, t:t + 1])
                        else:
                            ins = nc.vector.tensor_tensor_reduce(hd.score(b, t), o, hd.bias(t), 1.0, -3e38,
                                                                 ALU.add, ALU.max, mx[:, b, t:t + 1])
                        if t:
                            ins.then_inc(s_free, 1)
                    dve.wait_ge(s_free, 3 * a + 3)
                    if hd.sink is None:
                        ins = nc.vector.tensor_scalar(nb[:, b, :], mx[:, b, :], -hd.scale, None, ALU.mult)
                    else:
                        ins = nc.vector.tensor_scalar(nb[:, b, :], mx[:, b, :], -hd.scale, nsink[:, hd.sink:hd.sink + 1],
                                                      ALU.mult, ALU.min)
                    ins.then_inc(nb_done, 1)

                def norm(i):
                    hd, a = heads[i], a0 + i
                    b = a % 2
                    dve.wait_ge(exp_done, a + 1)
                    if hd.sink is not None:
                        link(nc.vector.tensor_tensor(rs[:, b, :], rs[:, b, :], es[:, b, :], ALU.add))
                    link(nc.vector.reciprocal(ri[:, b, :], rs[:, b, :]))
                    for t in range(T):
                        ins = nc.vector.tensor_scalar(hd.score(b, t), hd.score(b, t), ri[:, b, t:t + 1], None, ALU.mult)
                    ins.then_inc(p_done, 1)

                outs = {}

                def gated(i):
                    hd = heads[i]
                    o = outs[i] = (group(), c.g)
                    rows = slice(hd.dst[3], hd.dst[3] + HD)
                    if hd.gate is not None:
                        groups_stored(dve, c.g - 1)
                        nc.vector.scalar_tensor_tensor(otmp[rows, :], o[0][0:HD, :], 0.5, G[rows, hd.gate, :],
                                                       ALU.mult, ALU.mult)\
                            .then_inc(g_tmp, 1)

                def rest(i):
                    hd = heads[i]
                    h, l, ch, r0 = hd.dst
                    o, g = outs[i]
                    rows = slice(r0, r0 + HD)
                    src = o[0:HD, :] if hd.gate is None else otmp[rows, :]
                    lo(l[rows, ch, :], src, h[rows, ch, :]).then_inc(bank_free[(g - 1) % 2], 1)

                maxima(0)
                for i in range(len(heads)):
                    norm(i)
                    if i >= 2:
                        rest(i - 2)
                    if between:
                        between(i)
                    if i + 1 < len(heads):
                        maxima(i + 1)
                    if i:
                        gated(i - 1)
                rest(len(heads) - 2)
                gated(len(heads) - 1)
                rest(len(heads) - 1)
                c.head += len(heads)

            def low(t):
                ts = slice(t * P, (t + 1) * P)
                for half in range(2):
                    dve.wait_ge(xt_hi, c.xt + 1)
                    c.xt += 1
                    ks = slice(4 * half, 4 * half + 4)
                    nc.vector.tensor_tensor(XTl[:, ks, ts], bank[2 * t + half][:, :].rearrange("p (k n) -> p k n", k=4),
                                            XTh[:, ks, ts].bitcast(F32), ALU.subtract).then_inc(xt_lo, 1)

            def tail(make, norm=None):
                lag = 2 if norm else 1
                for t in range(T + lag):
                    if t < T:
                        if t and not norm:
                            dve.wait_ge(src_done, c.src)
                        make(t)
                        c.src += 1
                    if norm and 0 < t <= T:
                        norm(t - 1)
                    if t >= lag:
                        low(t - lag)

            def y_of(t):
                return banks[:, 2 * t:2 * t + 2, :].rearrange("p a b -> p (a b)")

            xt0 = [0]

            def h_norm(t, gain):
                r = inverse()
                if t:
                    dve.wait_ge(xt_done, xt0[0] + 2 * t)
                nc.vector.scalar_tensor_tensor(HT, x_tok[:, t, :], r, gain, ALU.mult, ALU.mult).then_inc(src_done, 1)

            def ln_tail(i):
                xt0[0] = c.xt

                def make(t):
                    if t == 0:
                        dve.wait_ge(vec_in[i], 16 * (3 if i == 3 else 2))
                    elif i == 3:
                        dve.wait_ge(x_new, t)
                    dve.wait_ge(y_done, c.tile + 1)
                    c.tile += 1
                    ins = nc.vector.scalar_tensor_tensor(YT, x_tok[:, t, :], ALPHA, y_of(t), ALU.mult, ALU.add)
                    link(ins)
                    nc.vector.bn_stats(st[:, 0, :], YT[:, 0:S])
                    link(nc.vector.bn_stats(st[:, 1, :], YT[:, S:D]))
                    nc.vector.bn_aggr(mv[:, :], st[:, :, :].rearrange("p a b -> p (a b)")).then_inc(ln_var, 1)
                    c.ln += 1
                    dve.wait_ge(ln_var, c.ln)
                    link(nc.vector.scalar_tensor_tensor(YT, YT, mv[:, 0:1], vec[0], ALU.subtract, ALU.mult))
                    r = inverse()
                    ins = nc.vector.scalar_tensor_tensor(x_tok[:, t, :], YT, r, vec[1], ALU.mult, ALU.add)
                    if i == 3:
                        ins.then_inc(x_new, 1)
                    else:
                        ins.then_inc(src_done, 1)
                tail(make, (lambda t: h_norm(t, V[:, :, :].rearrange("p a b -> p (a b)"))) if i == 3 else None)

            def rms_tail(n, last_saved=False):
                xt0[0] = c.xt

                def make(t):
                    if t == 0:
                        dve.wait_ge(vec_in[n], 32)
                    else:
                        dve.wait_ge(x_new, T * (n - 3) + t)
                    src = y_of(t)
                    c.tile += 1
                    if last_saved and t == T - 1:
                        dve.wait_ge(y_done, c.tile)
                        nc.vector.tensor_tensor(YT, src, Y3, ALU.add).then_inc(y_sum, 1)
                        src = YT
                    r = inverse()
                    ins = nc.vector.scalar_tensor_tensor(YT, src, r, vec[0], ALU.mult, ALU.mult)
                    link(ins)
                    nc.vector.tensor_tensor(x_tok[:, t, :], x_tok[:, t, :], YT, ALU.add).then_inc(x_new, 1)
                tail(make, lambda t: h_norm(t, vec[1]))

            def mla(j):
                c.g += 5
                dve.wait_ge(rope_in[j], 16)
                rotated(*rotate(0), 4, nope=False)
                groups_stored(dve, c.g)
                for s in range(3):
                    nc.vector.tensor_copy(QKl[HD:QH, 5 + s, :], QKl[HD:QH, 4, :].bitcast(F32)).then_inc(kr_done, 1)
                o = group()
                r = inverse(2 * T)
                stored(nc.vector.tensor_copy(nt[:, :], r[:, 0:1]))
                for n in range(2 * T):
                    ins = nc.vector.tensor_scalar(DIAG[:, n, :], ident[:, :], r[:, n:n + 1], None, ALU.mult)
                ins.then_inc(diag, 1)
                for i in MLA_GATES[0][:2]:
                    gate(i)
                for i0, n in ((0, 3), (3, 2)):
                    o = group()
                    for i in range(i0, i0 + n):
                        ins = nc.vector.scalar_tensor_tensor(G[:, i, :], G[:, i, :], qg[:, j, i:i + 1], o[:, :],
                                                             ALU.mult, ALU.mult)
                        ins.then_inc(c_tmp, 1)
                    dve.wait_ge(c_tmp, 5 * j + i0 + n)
                    stored(nc.vector.memset(nt[:, :], 0.0))
                for i in range(5):
                    dve.wait_ge(c_hi, 5 * j + i + 1)
                    nc.vector.tensor_tensor(OTl[:, i, :], G[:, i, :], OTh[:, i, :].bitcast(F32), ALU.subtract).then_inc(c_lo, 1)
                for i in MLA_GATES[0][2:]:
                    gate(i)

                def queries(h):
                    slots_free(h - 3)
                    groups_stored(dve, c.g)
                    outs = [rotate(0), rotate(1)]
                    for i in range(2):
                        rotated(*outs[i], (h + i) % GROUP)

                def keys_values(h):
                    slots_free(h - 1)
                    for p2 in range(2):
                        pair(4 + 2 * p2)
                    c.g += 2

                def between(i):
                    g, step = i // GROUP + 1, i % GROUP
                    if g == GROUP:
                        return
                    if step == 0:
                        queries(GROUP * g)
                    gates = MLA_GATES[1].get(g, ())
                    if step < len(gates):
                        gate(gates[step])
                    if step == 2:
                        keys_values(GROUP * g)
                    if step == 3:
                        queries(GROUP * g + 2)

                queries(0)
                keys_values(0)
                queries(2)
                attention(mla_heads(), between)
                ln_tail(3 * j)

            for t in range(T):
                low(t)
            dve.wait_ge(cst, N_CST)
            dve.wait_ge(ident_in, 16)
            nc.vector.tensor_scalar(nsink[:, :], sink[:, :], -1.0, None, ALU.mult)
            c.g += 2
            mla(0)
            for i in range(2):
                pair(4 + 2 * i)
            c.g += 2
            dve.wait_ge(win_in, 16)

            def between(i):
                if i < HEADS - GROUP:
                    if i % 2 == 0:
                        slots_free(i + 1)
                        pair((i + GROUP) % GROUP)
                    else:
                        gate((i + GROUP) // 2)

            for i in range(GROUP):
                between(i - GROUP)
            attention(swa_heads(), between)
            ln_tail(1)
            c.g += 1
            nc.vector.memset(OTh[32:64, 7, :].bitcast(F32), 1.0).then_inc(fx_m, 1)
            nc.vector.memset(OTl[32:64, 7, :].bitcast(F32), 0.0).then_inc(fx_m, 1)
            dve.wait_ge(own, 3)
            nc.vector.scalar_tensor_tensor(FL, FZ, 0.0, FA, ALU.min, ALU.subtract).then_inc(fx, 1)
            c.g += 1
            o = group()
            c.hi += 2
            dve.wait_ge(g_hi, c.hi)
            for ch, s in ((7, 1.0 / SCALE), (6, -1.0 / SCALE)):
                ins = nc.vector.scalar_tensor_tensor(OTl[0:HEADS, ch, :], o[0:HEADS, :], s, OTh[0:HEADS, ch, :].bitcast(F32),
                                                     ALU.mult, ALU.subtract)
            stored(ins)

            def between(i):
                if i < HEADS - GROUP:
                    step = i % GROUP
                    if step % 2 == 0:
                        slots_free(i + 1)
                        for slot in (step, 4 + step):
                            pair(slot)
                    elif step == 1:
                        c.g += 2
                    else:
                        gate((i + GROUP) // 2 - 1)
                        gate((i + GROUP) // 2)

            for i in range(GROUP):
                between(i - GROUP)
            attention(fox_heads(), between)
            ln_tail(2)
            mla(1)
            o = group()
            stored(lo(QKl[:, 4, :], o[:, :], QKh[:, 4, :]))
            c.g += 1
            for i in range(4):
                o = group()
                stored(lo(QKl[:, i, 0:S - P], o[:, 0:S - P], QKh[:, i, 0:S - P]))
            groups_stored(dve, c.g)
            for t in range(1, T):
                for h in range(IDX_HEADS):
                    n = c.idx
                    dve.wait_ge(idx_r, n + 1)
                    r = RELU[n % 2][:, 0:CAUSAL_KEYS[t]]
                    if h == 0:
                        ins = nc.vector.tensor_scalar(WORK[t], r, iw_t[:, t - 1, h:h + 1], None, ALU.mult)
                    else:
                        dve.wait_ge(idx_f, n)
                        ins = nc.vector.scalar_tensor_tensor(WORK[t], r, iw_t[:, t - 1, h:h + 1], WORK[t], ALU.mult, ALU.add)
                    ins.then_inc(idx_f, 1)
                    c.idx += 1
                dve.wait_ge(idx_f, c.idx)
                link(nc.vector.scalar_tensor_tensor(WORK[t], WORK[t], IDX_SCALE, zmask[:, S - CAUSAL_KEYS[t]:S],
                                                    ALU.mult, ALU.add))
            rounds = [t for t in range(1, T) for _ in range(TOPK // 8)]

            def top(n):
                for _ in range(min(n, len(rounds))):
                    t = rounds.pop(0)
                    link(nc.vector.max(top8[:, :], WORK[t]))
                    link(nc.vector.match_replace(WORK[t], top8[:, :], WORK[t], TAKEN))

            nc.vector.memset(PB[:, 2446:2448], 0.0)
            for cc in range(2):
                c.g += 1
                top(3)
                o = group()
                groups_stored(dve, c.g - 1)
                stored(nc.vector.tensor_tensor(CONV_H[:, 2:514], o[:, :], CONV_A, ALU.mult))
                groups_stored(dve, c.g)
                top(3)
                link(nc.vector.tensor_scalar(CONV_Y, CONV_H[:, 0:512], conv_w[:, cc, 0:1], None, ALU.mult))
                for tap in (1, 2):
                    link(nc.vector.scalar_tensor_tensor(CONV_Y, CONV_H[:, tap:tap + 512], conv_w[:, cc, tap:tap + 1], CONV_Y,
                                                        ALU.mult, ALU.add))
                o = group()
                groups_stored(dve, c.g - 1)
                nc.vector.tensor_tensor(otmp[:, :], o[:, :], CONV_Y, ALU.mult).then_inc(g_tmp, 1)
                stored(lo(OTl[:, cc, :], otmp[:, :], OTh[:, cc, :]))
            for b in range(3):
                ins = nc.vector.memset(POOL_B[b][:, 0:16], 0.0)
            ins.then_inc(pool_r, 1)
            dve.wait_ge(pool_in, 80)
            for cc in range(2):
                c.g += 1
                groups_stored(dve, c.g)
                v0, b1, b2 = POOL_B

                def doubled(dst, src, by):
                    link(nc.vector.tensor_tensor(dst[:, 16:528], src[:, 16:528], src[:, 16 - by:528 - by], ALU.add))

                doubled(b1, v0, 1)
                doubled(b2, b1, 2)
                if cc:
                    doubled(b1, b2, 4)
                    doubled(b2, b1, 8)
                for b, rows in ((b1, slice(0, HD)), (b2, slice(HD, P))):
                    link(nc.vector.tensor_tensor(b[rows, 16:528], b[rows, 16:528], V2[rows, cc, :], ALU.mult))
                    ins = nc.vector.tensor_tensor(v0[rows, 16:528], b[rows, 16:528], v0[rows, 16:528], ALU.subtract)
                ins.then_inc(pool_d, 1)
                o = group()
                groups_stored(dve, c.g - 1)
                if cc:
                    nc.vector.tensor_scalar(otmp[:, :], o[:, :], pool_s[:, cc:cc + 1], None, ALU.mult).then_inc(g_tmp, 1)
                else:
                    nc.vector.tensor_scalar(otmp[:, :], o[:, :], pool_s[:, cc:cc + 1], None, ALU.mult).then_inc(g_tmp, 1)
                    nc.vector.memset(POOL_B[0][:, 0:16], 0.0).then_inc(pool_r, 1)
                stored(lo(OTl[:, 2 + cc, :], otmp[:, :], OTh[:, 2 + cc, :]))
                top(5)
            dve.wait_ge(rel_in, 16 * 8)

            def between(i):
                if i < GROUP:
                    step = i % GROUP
                    if step % 2 == 0:
                        slots_free(i + 1)
                        for slot in (step, 4 + step):
                            pair(slot)
                            top(3)
                    elif step == 1:
                        c.g += 2
                        top(4)
                    if i == GROUP - 2:
                        top(48)
                        link(nc.vector.tensor_scalar(misc[:, :], misc[:, :], TAKEN / 2, NEG, ALU.is_gt, ALU.mult))
                    elif i >= 0:
                        top(3)

            for i in range(GROUP):
                between(i - GROUP)
            attention(rel_heads(), between)
            rms_tail(4)
            for lo_m, hi_m in ((0, KF_A), (KF_A, KF)):
                for m in range(lo_m, hi_m):
                    c.g += 1
                    o = group()
                    groups_stored(dve, c.g - 1)
                    h, l, ch = ff_dst[m]
                    nc.vector.tensor_tensor(otmp[:, :], o[:, :], SG[m % 2], ALU.mult).then_inc(g_tmp, 1)
                    stored(lo(l[:, ch, :], otmp[:, :], h[:, ch, :]))
            dve.wait_ge(y3, 2)
            rms_tail(5, last_saved=True)
            for cc in range(2):
                o = group()
                stored(lo(QKl[:, cc, :], o[:, :], QKh[:, cc, :]))
            for t in range(T):
                dve.wait_ge(ple_sg, t + 1)
                if t:
                    dve.wait_ge(fin, t)
                dve.wait_ge(y_done, c.tile + min(2 * t + 3, 2 * T))
                for half in range(2):
                    hs = slice(half * S, half * S + S)
                    ins = nc.vector.tensor_tensor(YT[:, hs], bank[2 * t + half][:, :], G[:, 2 * t + half, :], ALU.mult)
                link(ins)
                nc.vector.tensor_tensor(x_tok[:, t, :], x_tok[:, t, :], YT, ALU.add).then_inc(fin, 1)

        @block.gpsimd
        def _(pool):
            for dst, src in CONSTANTS:
                pool.dma_start(dst, src).then_inc(cst, 16)
            pool.memset(eps[:, 0:1], RMS_EPS)
            pool.memset(eps[:, 1:2], LN_EPS)
            pool.memset(ones[:, :], 1.0).then_inc(pool_cst, 1)
            pool.wait_ge(pool_cst, 1)
            pool.memset(rel_t[BUCKETS:BUCKETS + 1, :], 1.0).then_inc(pool_cst, 1)
            pool.dma_start(REL_1H, consts["onehot"]).then_inc(onehot_in, 16)
            pool.dma_start(misc[HD:P, 0:S], consts["rope"]).then_inc(rope_in[0], 16)

            def fix(u):
                if u < NU and units[u][4]:
                    _, nk, ncol, _, _ = units[u]
                    pool.wait_ge(raw_in[u % RAW], raw_at[u])
                    v = w_raw[:, u % RAW, 0:nk * ncol].rearrange("p (a n) -> p a n", n=P)
                    pool.tensor_copy(v[:, :, QH:QH + 16], v[:, :, HD + 16:QH]).then_inc(fixed, 1)
                    pool.tensor_copy(v[:, :, QH + 16:P], v[:, :, HD:HD + 16]).then_inc(fixed, 1)

            pool.wait_ge(pool_cst, 2)
            fix(0)
            for u in range(NU):
                fix(u + 1)
                pool.wait_ge(hi_done, u + 1)
                pool.tensor_tensor(view(w_lo, u, RING), view(w_raw, u, RAW), view(w_hi, u, RING).bitcast(F32),
                                   ALU.subtract).then_inc(lo_done, 1)


_INS = ["x", "ln_g", "ln_b", "mla_w_in", "mla_q_norm", "mla_w_q_up", "mla_kv_norm", "mla_w_kv_up", "mla_w_out",
        "swa_w_in", "swa_sinks", "swa_w_out", "fox_w_in", "fox_b_f", "fox_w_out", "p_2", "rel_bias_2", "g_mix_pre_2",
        "w_in_2", "conv_w_2", "pool_w_2", "pool_scale_2", "w_out_2", "g_mix_post_2", "g_ffn_pre_2", "w_gate_up_2",
        "w_down_2", "g_ffn_post_2", "g_ple_2", "w_ple_gate_2", "w_ple_proj_2"]


def tables():
    f = np.float32
    q, k = np.arange(P)[:, None], np.arange(P)[None, :]
    zmask = np.zeros((P, S), f)
    zmask[:, S - P:] = np.where(k <= q, f(0), f(NEG))
    tri = np.ones((P, S), f)
    tri[:, 0:P] = (k >= q).astype(f)
    inv = f(10000.0) ** (-np.arange(0, ROPE, 2, dtype=f) / f(ROPE))
    ang = (np.arange(S, dtype=f)[:, None] * inv[None, :]).T.astype(f)
    cos, sin = np.cos(ang).astype(f), np.sin(ang).astype(f)
    rope = np.concatenate([cos, cos, -sin, sin])
    dist = q + P - np.arange(2 * P)[None, :]
    window = np.where((dist >= 0) & (dist < P), dist, BIG).astype(f)
    counts = np.zeros((P, 2, S), f)
    for i, n in enumerate((2, 4, 8, 16)):
        counts[HD * (i % 2):HD * (i % 2) + HD, i // 2, :] = f(1) / np.minimum(np.arange(S) + 1, n).astype(f)
    d = S - 1 - np.arange(REL_L)
    exact = BUCKETS // 2
    large = exact + (np.log(np.maximum(d, 1).astype(f) / f(exact)) / f(np.log(P / exact)) * f(BUCKETS - exact)).astype(np.int32)
    bucket = np.where(d < exact, np.maximum(d, 0), np.minimum(large, BUCKETS - 1))
    onehot = np.zeros((BUCKETS + 1, REL_L), f)
    onehot[bucket[d >= 0], np.nonzero(d >= 0)[0]] = 1.0
    onehot[BUCKETS, d < 0] = NEG
    return {"ident": np.eye(P, dtype=f), "zmask": zmask, "tri": tri, "rope": rope, "window": window, "counts": counts,
            "onehot": onehot}


def kernel(**inputs):
    cols = {n: np.asarray(inputs[n]) for n in ("mla_q_norm", "mla_kv_norm", "fox_b_f", "pool_scale_2", "rel_bias_2", "conv_w_2")}
    inputs = dict(inputs)
    inputs["mla_q_norm"] = cols["mla_q_norm"].reshape(2, 3, P).transpose(2, 0, 1)
    inputs["mla_kv_norm"] = cols["mla_kv_norm"].reshape(2, 2, P).transpose(2, 0, 1)
    inputs["fox_b_f"] = cols["fox_b_f"].reshape(HEADS, 1)
    inputs["pool_scale_2"] = cols["pool_scale_2"].reshape(2, P).T
    inputs["rel_bias_2"] = cols["rel_bias_2"].T
    inputs["conv_w_2"] = cols["conv_w_2"].reshape(3, 2, P).transpose(2, 1, 0)
    import concourse.bacc as _bacc
    from concourse.bass_utils import run_bass_kernel_spmd as _run

    nc = _bacc.Bacc("TRN2", target_bir_lowering=False, num_devices=1)
    arrays, w, consts = {}, {}, {}
    for group, names in ((w, {n: inputs[n] for n in _INS}), (consts, tables())):
        for name, value in names.items():
            a = np.ascontiguousarray(value)
            arrays[f"in_{name}_dram"] = a
            group[name] = nc.dram_tensor(f"in_{name}_dram", a.shape, mybir.dt.from_np(a.dtype), kind="ExternalInput").ap()
    out = nc.dram_tensor("out_dram", (1, S, D), F32, kind="ExternalOutput").ap()
    build(nc, w, consts, out)
    r = _run(nc, [arrays], core_ids=[0])
    return r.results[0]["out_dram"]
```
